# Optimizing a Trainium2 kernel written in Bass

```python
import jax, jax.numpy as jnp
from jax import lax
import numpy as np

D_MODEL = 1024
BATCH = 1
SEQ = 1024
DEPTH = 1

CHUNK = 64
MIX_WIDTH = D_MODEL
HG_HEADS = 4
HG_WIDTH = MIX_WIDTH // 2
HG_HEAD_DIM = HG_WIDTH // HG_HEADS
POOL_WINDOWS = (2, 4, 8, 16)
POOL_GROUPS = 4
POOL_WIDTH = MIX_WIDTH - HG_WIDTH
POOL_GDIM = POOL_WIDTH // POOL_GROUPS
IN_WIDTH = 4 * HG_WIDTH + POOL_WIDTH
N_BRANCH = 2
MOE_GROUPS = 4
MOE_EXPERTS_PER_GROUP = 8
N_EXPERTS = MOE_GROUPS * MOE_EXPERTS_PER_GROUP
MOE_TOP_K = 2
EXPERT_FF = D_MODEL // 2
MOE_BLOCK = 256
EPS = 1e-6
ADA_INIT = 0.5

kernel_name = "hybrid_hgrn2_pool_hmoe_block"

def rms_norm(x, g):
    xf = x.astype(jnp.float32)
    y = xf * lax.rsqrt(jnp.mean(xf * xf, axis=-1, keepdims=True) + EPS)
    return (y * g.astype(jnp.float32)).astype(x.dtype)

def hgrn2_mixer(q_raw, f_raw, v_raw, g_raw, lb, norm_g):
    f32 = jnp.float32
    Bsz, S, _ = q_raw.shape
    nC = S // CHUNK
    heads = lambda t: t.astype(f32).reshape(Bsz, S, HG_HEADS, HG_HEAD_DIM)
    q = jax.nn.silu(heads(q_raw))
    lbh = lb.astype(f32).reshape(HG_HEADS, HG_HEAD_DIM)
    f = lbh + (1.0 - lbh) * jax.nn.sigmoid(heads(f_raw))
    k = 1.0 - f
    log_f = jnp.log(f)

    def chunks(t):
        return t.reshape(Bsz, nC, CHUNK, HG_HEADS, HG_HEAD_DIM).transpose(1, 0, 3, 2, 4)

    qc, kc, vc = chunks(q), chunks(k), chunks(heads(v_raw))
    bc = jnp.cumsum(chunks(log_f), axis=3)
    causal = jnp.tril(jnp.ones((CHUNK, CHUNK), bool))[:, :, None]

    def step(state, inp):
        qb, kb, vb, bb = inp
        diff = bb[:, :, :, None, :] - bb[:, :, None, :, :]
        decay = jnp.exp(jnp.where(causal, diff, -jnp.inf))
        scores = jnp.sum(qb[:, :, :, None, :] * kb[:, :, None, :, :] * decay, axis=-1)
        o = (jnp.einsum('bhts,bhsv->bhtv', scores, vb)
             + jnp.einsum('bhtk,bhkv->bhtv', qb * jnp.exp(bb), state))
        b_last = bb[:, :, -1:, :]
        state = (jnp.exp(b_last[:, :, 0, :, None]) * state
                 + jnp.einsum('bhsk,bhsv->bhkv', kb * jnp.exp(b_last - bb), vb))
        return state, o

    s0 = jnp.zeros((Bsz, HG_HEADS, HG_HEAD_DIM, HG_HEAD_DIM), f32)
    _, o = lax.scan(step, s0, (qc, kc, vc, bc))
    o = o.transpose(1, 0, 3, 2, 4).reshape(Bsz, S, HG_HEADS, HG_HEAD_DIM)
    o = o * lax.rsqrt(jnp.mean(o * o, axis=-1, keepdims=True) + EPS)
    o = o.reshape(Bsz, S, HG_WIDTH) * norm_g.astype(f32) * jax.nn.silu(g_raw.astype(f32))
    return o.astype(q_raw.dtype)

def multiscale_pool(u, w_grp, ls):
    f32 = jnp.float32
    Bsz, S, _ = u.shape
    uf = u.astype(f32).reshape(Bsz, S, POOL_GROUPS, POOL_GDIM)
    cs = jnp.pad(jnp.cumsum(uf, axis=1), ((0, 0), (1, 0), (0, 0), (0, 0)))
    win = jnp.array(POOL_WINDOWS, jnp.int32)
    t = jnp.arange(S, dtype=jnp.int32)[:, None]
    lo = jnp.maximum(t + 1 - win[None, :], 0)
    grp = jnp.arange(POOL_GROUPS, dtype=jnp.int32)[None, :]
    window_sum = cs[:, 1:] - cs[:, lo, grp]
    count = jnp.minimum(t + 1, win[None, :]).astype(f32)
    pooled = window_sum / count[None, :, :, None] - uf
    mixed = jnp.einsum('bsgc,gcd->bsgd', pooled, w_grp.astype(f32)).reshape(Bsz, S, POOL_WIDTH)
    return (mixed * ls.astype(f32)).astype(u.dtype)

def hierarchical_moe(h, w_rg, b_rg, w_re, b_re, w_gate_e, w_up_e, w_down_e):
    f32 = jnp.float32
    Bsz, S, D = h.shape
    N = Bsz * S
    hf = h.reshape(N, D)
    p_g = jax.nn.softmax((hf @ w_rg + b_rg).astype(f32), axis=-1)
    p_top_g, g_idx = lax.top_k(p_g, 1)
    e_logits = (hf @ w_re + b_re).astype(f32).reshape(N, MOE_GROUPS, MOE_EXPERTS_PER_GROUP)
    e_sel = jnp.take_along_axis(e_logits, g_idx[:, :, None], axis=1)[:, 0]
    p_top_e, e_local = lax.top_k(jax.nn.softmax(e_sel, axis=-1), MOE_TOP_K)
    weights = p_top_g * p_top_e / jnp.sum(p_top_e, axis=-1, keepdims=True)
    e_global = g_idx * MOE_EXPERTS_PER_GROUP + e_local

    A = N * MOE_TOP_K
    e_flat = e_global.reshape(A).astype(jnp.int32)
    tok_flat = jnp.repeat(jnp.arange(N, dtype=jnp.int32), MOE_TOP_K)
    w_flat = weights.reshape(A)
    order = jnp.argsort(e_flat)
    e_sorted = e_flat[order]
    counts = jnp.bincount(e_flat, length=N_EXPERTS)
    pcounts = ((counts + MOE_BLOCK - 1) // MOE_BLOCK) * MOE_BLOCK
    start = jnp.cumsum(counts) - counts
    pend = jnp.cumsum(pcounts)
    pstart = pend - pcounts
    dest = pstart[e_sorted] + jnp.arange(A, dtype=jnp.int32) - start[e_sorted]
    n_blocks = -(-A // MOE_BLOCK) + N_EXPERTS
    P = n_blocks * MOE_BLOCK
    row_tok = jnp.full((P,), N, jnp.int32).at[dest].set(tok_flat[order])
    row_w = jnp.zeros((P,), f32).at[dest].set(w_flat[order])
    block_e = jnp.minimum(jnp.searchsorted(pend, jnp.arange(n_blocks) * MOE_BLOCK, side='right'),
                          N_EXPERTS - 1).astype(jnp.int32)
    x_pad = jnp.concatenate([hf, jnp.zeros((1, D), hf.dtype)], axis=0)
    xb = x_pad[row_tok].reshape(n_blocks, MOE_BLOCK, D)

    def expert_block(args):
        xblk, e = args
        return (jax.nn.silu(xblk @ w_gate_e[e]) * (xblk @ w_up_e[e])) @ w_down_e[e]

    yb = lax.map(expert_block, (xb, block_e))
    y = jax.ops.segment_sum(yb.reshape(P, D).astype(f32) * row_w[:, None], row_tok,
                            num_segments=N + 1)[:N]
    return y.reshape(Bsz, S, D).astype(h.dtype)

def setup_inputs(seed: int = 0) -> dict:
    key = jax.random.key(seed)
    ks = jax.random.split(key, 26)
    f32 = jnp.float32
    D = D_MODEL

    def nrm(k, shape, scale):
        return scale * jax.random.normal(k, shape, f32)

    return {
        "x": nrm(ks[0], (BATCH, SEQ, D), 1.0),
        "c": nrm(ks[1], (BATCH, D), 1.0),
        "w_ada": nrm(ks[2], (DEPTH, D, 6 * D), ADA_INIT * D ** -0.5),
        "b_ada": nrm(ks[3], (DEPTH, 6 * D), 0.02),
        "g_pre_mix": 1.0 + nrm(ks[4], (DEPTH, D), 0.02),
        "g_post_mix": 1.0 + nrm(ks[5], (DEPTH, D), 0.02),
        "w_in": nrm(ks[6], (DEPTH, D, IN_WIDTH), D ** -0.5),
        "hg_lb_logits": nrm(ks[7], (DEPTH + 1, HG_WIDTH), 0.1),
        "hg_norm_g": 1.0 + nrm(ks[8], (DEPTH, HG_WIDTH), 0.02),
        "pool_w": nrm(ks[9], (DEPTH, POOL_GROUPS, POOL_GDIM, POOL_GDIM), POOL_GDIM ** -0.5),
        "pool_scale": 1.0 + nrm(ks[10], (DEPTH, POOL_WIDTH), 0.02),
        "w_branch_hg": nrm(ks[11], (DEPTH, HG_WIDTH, D), HG_WIDTH ** -0.5),
        "w_branch_pool": nrm(ks[12], (DEPTH, POOL_WIDTH, D), POOL_WIDTH ** -0.5),
        "w_gate": nrm(ks[13], (DEPTH, D, N_BRANCH * D), D ** -0.5),
        "b_gate": nrm(ks[14], (DEPTH, N_BRANCH * D), 0.02),
        "w_out": nrm(ks[15], (DEPTH, D, D), D ** -0.5),
        "g_pre_ffn": 1.0 + nrm(ks[16], (DEPTH, D), 0.02),
        "g_post_ffn": 1.0 + nrm(ks[17], (DEPTH, D), 0.02),
        "w_router_group": nrm(ks[18], (DEPTH, D, MOE_GROUPS), D ** -0.5),
        "b_router_group": nrm(ks[19], (DEPTH, MOE_GROUPS), 0.01),
        "w_router_expert": nrm(ks[20], (DEPTH, D, N_EXPERTS), D ** -0.5),
        "b_router_expert": nrm(ks[21], (DEPTH, N_EXPERTS), 0.01),
        "w_exp_gate": nrm(ks[22], (DEPTH, N_EXPERTS, D, EXPERT_FF), D ** -0.5),
        "w_exp_up": nrm(ks[23], (DEPTH, N_EXPERTS, D, EXPERT_FF), D ** -0.5),
        "w_exp_down": nrm(ks[24], (DEPTH, N_EXPERTS, EXPERT_FF, D), EXPERT_FF ** -0.5),
    }

def reference(x, c, w_ada, b_ada, g_pre_mix, g_post_mix, w_in, hg_lb_logits, hg_norm_g, pool_w,
              pool_scale, w_branch_hg, w_branch_pool, w_gate, b_gate, w_out, g_pre_ffn, g_post_ffn,
              w_router_group, b_router_group, w_router_expert, b_router_expert, w_exp_gate,
              w_exp_up, w_exp_down):
    lb_all = jnp.cumsum(jax.nn.softmax(hg_lb_logits.astype(jnp.float32), axis=0), axis=0)
    cond = jax.nn.silu(c)
    h = x
    for l in range(DEPTH):
        ada = (cond @ w_ada[l] + b_ada[l])[:, None, :]
        sh1, sc1, gt1, sh2, sc2, gt2 = jnp.split(ada, 6, axis=-1)

        hn = rms_norm(h, g_pre_mix[l]) * (1.0 + sc1) + sh1
        proj = hn @ w_in[l]
        q, f, i, g, u = jnp.split(proj, [HG_WIDTH, 2 * HG_WIDTH, 3 * HG_WIDTH, 4 * HG_WIDTH], axis=-1)
        y_hg = hgrn2_mixer(q, f, i, g, lb_all[l], hg_norm_g[l]) @ w_branch_hg[l]
        y_pool = multiscale_pool(u, pool_w[l], pool_scale[l]) @ w_branch_pool[l]
        gate_hg, gate_pool = jnp.split(jax.nn.sigmoid(hn @ w_gate[l] + b_gate[l]), 2, axis=-1)
        mix = (gate_hg * y_hg + gate_pool * y_pool) @ w_out[l]
        h = h + gt1 * rms_norm(mix, g_post_mix[l])

        hn = rms_norm(h, g_pre_ffn[l]) * (1.0 + sc2) + sh2
        y = hierarchical_moe(hn, w_router_group[l], b_router_group[l], w_router_expert[l],
                             b_router_expert[l], w_exp_gate[l], w_exp_up[l], w_exp_down[l])
        h = h + gt2 * rms_norm(y, g_post_ffn[l])
    return h


_drawn_inputs = setup_inputs


def setup_inputs(seed=0):
    import zlib

    import numpy as np

    out = dict(_drawn_inputs(seed))
    spreads = {}
    factors = {'hg_lb_logits': 4.889,
     'hg_norm_g': 2.8,
     'pool_scale': 2.704,
     'b_gate': 3.454,
     'g_post_ffn': 8.0,
     'b_router_group': 2.951,
     'b_router_expert': 3.669}
    for name, (base, spread) in spreads.items():
        noise = np.random.default_rng([zlib.crc32(name.encode()), seed]).standard_normal(out[name].shape)
        drawn = base * np.exp(spread * noise) if base else spread * noise
        out[name] = __import__('jax').numpy.asarray(drawn.astype(out[name].dtype))
    for name, factor in factors.items():
        out[name] = (out[name] * factor).astype(out[name].dtype)
    return out
```

```python
from contextlib import ExitStack

import concourse.bass as bass
from concourse import mybir

F32 = mybir.dt.float32
F32R = mybir.dt.float32r
I32 = mybir.dt.int32
ALU = mybir.AluOpType
ACT = mybir.ActivationFunctionType
AX = mybir.AxisListType

P = 128
D = 1024
S = 1024
KC = D // P
NT = S // P
HALF = 512
H = 4
EPS = 1e-6
G, EG = 4, 8
E = G * EG
FF = 512
BLK = 128
NJ = (S - 1) // BLK
NOV = (2 * S - 1) // BLK
NCOL = E + NOV
LEVELS = [1, 2, 4, 8, 16, 32, 64]
KB = 1024

W_IN_ORDER = [4, 8, 16, 0, 12]
N_IN = 20
N_A = N_IN + 16
N_CH = N_A + KC

C_COND, C_BADA, C_GPRE, C_BGATE, C_LB0, C_LB1, C_NG, C_PS, N_VEC = 0, 8, 24, 32, 48, 52, 56, 60, 64


class Chain:

    def __init__(self, eng, sem):
        self.eng, self.sem, self.n, self.steps = eng, sem, 0, 0

    def link(self, ins):
        self.n = self.n + 1
        self.steps += 1
        ins.then_inc(self.sem, 1)
        self.eng.wait_ge(self.sem, self.n)

    def enter(self, i, per, first=0):
        self.base, self.per, self.steps = self.n - first * per, per, 0
        self.n = i * per + self.base

    def leave(self, end):
        assert self.steps == self.per, (self.steps, self.per)
        self.n = self.base + end * self.per


def past(eng, sem, count):
    if not (isinstance(count, int) and count <= 0):
        eng.wait_ge(sem, count)


def build(nc, x, c, w_ada, b_ada, g_pre_mix, g_post_mix, w_in, lb_logits, hg_norm_g, pool_w, pool_scale,
          w_bhg, w_bpool, w_gate, b_gate, w_out, g_pre_ffn, g_post_ffn, w_rg, b_rg, w_re, b_re,
          w_eg, w_eu, w_ed, out):
    with ExitStack() as ctx:
        def at(name, shape, dt, kb):
            return nc.alloc_sbuf_tensor_at(name, shape, dt, offset=int(kb * KB))

        def sem(name):
            return ctx.enter_context(nc.semaphore(name))

        def dram(name, shape):
            return nc.dram_tensor(name, shape, F32, kind="Internal").ap()

        o = -(-nc.sbuf_base // KB)
        ident = at("ident", [P, P], F32, o + 0)
        ones = at("ones", [P, P], F32, o + 0.5)
        mask = at("mask", [P, 7, 64], I32, o + 1)
        cols = at("cols", [P, N_VEC], F32, o + 2.75)
        small = at("small", [P, 192], F32, o + 3)
        valr = at("valr", [P, 2, HALF], F32, o + 4)
        win2 = at("win2", [P, S], F32, o + 4)
        rowr = at("rowr", [1, HALF], F32, o + 8)
        hnh = at("hnh", [P, KC, S], F32R, o + 10)
        hnl = at("hnl", [P, KC, S], F32R, o + 42)
        raw = at("raw", [P, 2, KC, P], F32, o + 74)
        wh = at("wh", [P, 2, KC, P], F32R, o + 82)
        wl = at("wl", [P, 2, KC, P], F32R, o + 90)
        xt = at("xt", [P, NT, D], F32, o + 98)
        adab = at("adab", [P, 4, 4, HALF], F32, o + 130)
        acc0 = at("acc0", [P, 4, HALF], F32, o + 162)
        acc1 = at("acc1", [P, 2, HALF], F32, o + 170)
        vecs = at("vecs", [N_VEC, P], F32, o + 8)
        xorm = at("xorm", [P, P], I32, o + 174)
        iS = at("iS", [P, P], I32, o + 174.5)
        iT = at("iT", [P, P], I32, o + 175)
        mtmp = at("mtmp", [P, 64], F32, o + 175.5)
        Bc = at("Bc", [P, H, S], F32, o + 98)
        Kk = at("Kk", [P, H, S], F32, o + 114)
        Qq = at("Qq", [P, H, S], F32, o + 130)
        Vv = at("Vv", [P, NT, HALF], F32, o + 146)
        scanm = at("scanm", [P, S], F32, o + 162)
        win1 = at("win1", [P, S], F32, o + 166)
        vT = at("vT", [P, H, S], F32, o + 174)
        ub = at("ub", [P, H, S], F32, o + 190)
        gt = at("gt", [P, 2, S], F32, o + 194)
        poolw = at("poolw", [P, H, P], F32, o + 8)
        Dd = at("Dd", [P, 2, H, P], F32, o + 162)
        Ee = at("Ee", [P, 2, H, P], F32, o + 166)
        E0 = at("E0", [P, H, P], F32, o + 170)
        QL = at("QL", [P, 2, H, 64], F32, o + 172)
        KL = at("KL", [P, 2, H, P], F32, o + 174)
        Kc = at("Kc", [P, H, P], F32, o + 178)
        Sc = at("Sc", [P, H, P], F32, o + 180)
        qe = at("qe", [P, H, P], F32, o + 182)
        kd = at("kd", [P, H, P], F32, o + 184)
        kdN = at("kdN", [P, H, P], F32, o + 186)
        St = at("St", [P, H, P], F32, o + 188)
        on = at("on", [P, H, P], F32, o + 190)
        ov = at("ov", [P, H, P], F32, o + 192)
        gs = at("gs", [P, H, P], F32, o + 202)
        sqs = at("sqs", [P, H, P], F32, o + 204)
        oh = at("oh", [P, H, S], F32R, o + 98)
        ol = at("ol", [P, H, S], F32R, o + 114)
        mixr = at("mixr", [P, H, S], F32, o + 130)
        mh = at("mh", [P, H, S], F32R, o + 146)
        ml = at("ml", [P, H, S], F32R, o + 162)
        ghg = at("ghg", [P, 2, S], F32, o + 178)
        gpl = at("gpl", [P, 2, S], F32, o + 186)
        t12 = at("t12", [P, 2, HALF], F32, o + 202)
        woh = at("woh", [P, KC, D], F32R, o + 98)
        wol = at("wol", [P, KC, D], F32R, o + 130)
        rows = at("rows", [P, 4, D], F32, o + 162)
        rtmp = at("rtmp", [P, 2, D], F32, o + 82)
        xr = at("xr", [P, 2, D], F32, o + 178)
        hh = at("hh", [P, 2, D], F32, o + 186)
        hn2 = at("hn2", [P, 2, D], F32, o + 194)
        h2T = at("h2T", [P, KC, P], F32, o + 82)
        wr = at("wr", [P, KC, G + E], F32, o + 90)
        brow = at("brow", [P, G + E], F32, o + 91.5)
        junk = at("junk", [P, D], F32, o + 92)
        mm_t = at("mm_t", [P, D], F32, o + 202)
        L = at("L", [P, NT, G + E], F32, o + 96)
        R = [at(f"R{k}", [P, NT, G, EG], F32, o + 178 + k) for k in range(12)]
        rs_ = at("rs_", [P, 24, 2, NT], F32, o + 190)
        c32 = at("c32", [P, 8, E], F32, o + 192)
        iotaS = at("iotaS", [P, P], F32, o + 193)
        iotaC = at("iotaC", [P, 64], F32, o + 193.5)
        Aoh = at("Aoh", [P, 2, P], F32, o + 194)
        Boh = at("Boh", [P, 2, 64], F32, o + 195)
        tri = at("tri", [P, P], F32, o + 195.5)
        ovcmp = at("ovcmp", [P, NOV, E], F32, o + 196)
        wts = at("wts", [P, 2, NT], F32, o + 170)
        dest = at("dest", [P, 2, NT], I32, o + 170.25)
        idxt = at("idxt", [P, 64], I32, o + 170.5)
        idxc = at("idxc", [P, 2, 1], I32, o + 171)
        ovt = at("ovt", [1, 64], I32, o + 171.25)
        ovf = at("ovf", [1, 64], F32, o + 171.5)
        raw6 = at("raw6", [P, 6, 4, HALF], F32, o + 10)
        eh = at("eh", [P, 6, 4, HALF], F32R, o + 58)
        el = at("el", [P, 6, 4, HALF], F32R, o + 106)
        xTh = at("xTh", [P, 2, KC, P], F32R, o + 154)
        xTl = at("xTl", [P, 2, KC, P], F32R, o + 162)
        sil = at("sil", [P, HALF], F32, o + 172)
        xg = at("xg", [P, 2, D], F32, o + 178)
        aa = at("aa", [P, 2, HALF], F32, o + 186)
        aTh = at("aTh", [P, 2, 4, P], F32R, o + 190)
        aTl = at("aTl", [P, 2, 4, P], F32R, o + 194)
        yy = at("yy", [P, D], F32, o + 198)
        Y1 = at("Y1", [P, 2, D], F32, o + 10)
        Y2 = at("Y2", [P, 2, D], F32, o + 18)
        hb = at("hb", [P, 2, D], F32, o + 26)
        yo = at("yo", [P, 2, D], F32, o + 34)
        ysq = at("ysq", [P, D], F32, o + 42)

        A = [ctx.enter_context(nc.psum_tensor(f"bank{k}", [P, HALF], F32)) for k in range(8)]

        spill = dram("spill", (20 + 4, P, S))
        ada_d = dram("ada_d", (8, HALF))
        h_d = dram("h_d", (S, D))
        hn2_d = dram("hn2_d", (S, D))
        y_d = dram("y_d", (NCOL * BLK, D))

        xv = x.rearrange("b (t p) d -> t p (b d)", p=P)
        outv = out.rearrange("b (t p) d -> t p (b d)", p=P)
        adav = w_ada[0].rearrange("(k p) n -> p k n", p=P)
        winv = w_in[0].rearrange("(k p) n -> p k n", p=P)
        wgav = w_gate[0].rearrange("(k p) n -> p k n", p=P)
        wbh = w_bhg[0].rearrange("(k p) n -> p k n", p=P)
        wbp = w_bpool[0].rearrange("(k p) n -> p k n", p=P)
        wov = w_out[0].rearrange("(k p) n -> k p n", p=P)
        egv = w_eg[0].rearrange("e (k p) n -> e p k n", p=P)
        euv = w_eu[0].rearrange("e (k p) n -> e p k n", p=P)
        edv = w_ed[0].rearrange("e (k p) n -> e p k n", p=P)

        names = """s_vec s_vecT s_cols s_cond s_x s_ssq s_sd s_xs s_xT s_val s_hh s_hn s_ident s_ones s_acc
            s_mod s_modc s_adam s_rowc s_rowst s_raw0 s_raw1 s_hi s_lo s_mm s_free s_ln s_B s_vt s_ve s_pool
            s_pm s_pe s_lbx s_pw s_const s_mask s_kc s_E s_D s_qe s_kd s_QK s_sc s_mg s_kt s_kn s_st s_S s_o
            s_osq s_osd s_on s_ot s_oval s_oh s_ol s_gs s_mixr s_mh s_ml s_gl0 s_gl1 s_br s_bf s_bval s_mTh s_mTl
            s_worh s_worl s_rowl s_rows s_rowf s_xr0 s_xr1 s_wo s_mixsq s_mixsd s_mt s_h s_hst0 s_hst1 s_hsq
            s_hsd s_hn2 s_nst0 s_nst1 s_h2T s_h2e s_rt s_L s_wr s_ge s_M s_pos s_tab s_AB s_slots s_tabd s_iota
            s_idx s_xg0 s_xg1 s_xTp s_xTh s_xTl s_phi s_plo s_pc s_gu s_sil s_a s_aT s_aTh s_aTl
            s_y s_ycp s_yst s_Y0 s_Y1 s_hb0 s_hb1 s_ysum s_ysq s_ysd s_fin s_out0 s_out1 s_gst0 s_gst1
            s_ebl s_ovd s_dve s_act s_pool_own s_settled s_sg""".split()
        Z = {n: sem(n) for n in names}
        s_ada = [sem(f"s_ada{k}") for k in range(4)]
        s_r6 = [sem(f"s_r6_{k}") for k in range(6)]

        block = ctx.enter_context(nc.Block())

        def settle(eng):
            eng.sem_inc(Z["s_settled"], 1)

        def one(view):
            return view.rearrange("a p n -> p (a n)")

        @block.sync
        def _(sp):
            def vec(lo, n, src):
                sp.dma_start(vecs[lo:lo + n, :], src).then_inc(Z["s_vec"], 16)

            vec(C_COND, 8, c.rearrange("a (j p) -> (a j) p", p=P))
            vec(C_BADA, 16, b_ada[0:1, 0:2 * D].rearrange("a (j p) -> (a j) p", p=P))
            vec(C_GPRE, 8, g_pre_mix.rearrange("a (j p) -> (a j) p", p=P))
            vec(C_BGATE, 16, b_gate.rearrange("a (j p) -> (a j) p", p=P))
            vec(C_LB0, 8, lb_logits.rearrange("a (j p) -> (a j) p", p=P))
            vec(C_NG, 4, hg_norm_g.rearrange("a (j p) -> (a j) p", p=P))
            vec(C_PS, 4, pool_scale.rearrange("a (j p) -> (a j) p", p=P))

            def ada(piece, slot, first=False):
                for k in range(2):
                    if not first:
                        sp.wait_ge(Z["s_acc"], piece - 1)
                    sp.dma_start(adab[:, slot + k], adav[:, 4 * k:4 * k + 4, bass.ts(piece, HALF)]).then_inc(
                        s_ada[slot + k], 16)

            ada(0, 0, True)
            ada(1, 2, True)
            ada(2, 0)
            ada(3, 2)

            def chunk(cn, slot, top, bottom, wait=True):
                if wait:
                    sp.wait_ge(Z["s_lo"], cn - 1)
                sp.dma_start(raw[:, slot, 0:4], top).then_inc(Z[f"s_raw{slot}"], 16)
                sp.dma_start(raw[:, slot, 4:8], bottom).then_inc(Z[f"s_raw{slot}"], 16)

            def chunk_of(view, cn, slot, col, wait=True):
                chunk(cn, slot, view[:, 0:4, bass.ts(col, P)], view[:, 4:8, bass.ts(col, P)], wait)

            chunk_of(winv, 0, 0, W_IN_ORDER[0], False)
            chunk_of(winv, 1, 1, W_IN_ORDER[0] + 1, False)
            for cn in range(2, 10):
                chunk_of(winv, cn, cn % 2, W_IN_ORDER[cn // 4] + cn % 4)
                ada(cn + 2, 2 * (cn % 2))
            chunk_of(winv, 10, 0, W_IN_ORDER[2] + 2)
            chunk_of(winv, 11, 1, W_IN_ORDER[2] + 3)
            for kind in (3, 4):
                with sp.Fori(0, 4 // 2) as pair:
                    j = pair * 2
                    for b in range(2):
                        chunk_of(winv, j + (4 * kind + b), b, j + (W_IN_ORDER[kind] + b))
                if kind == 3:
                    sp.wait_ge(Z["s_rowst"], 16 * 8)
                    sp.dma_start(poolw[:], pool_w[0].rearrange("g p n -> p g n")).then_inc(Z["s_pw"], 16)
            def gates(t):
                for b in range(2):
                    chunk_of(wgav, t * 2 + (N_IN + b), b, t * 2 + b)
                sp.wait_ge(Z["s_gst0"], 16 * 4)
                sp.wait_ge(Z["s_gst1"], 16 * 4)
                past(sp, Z["s_oval"], t)
                sp.dma_start(gs[:], spill[4:8, :, bass.ts(t, P)].rearrange("h p n -> p h n")).then_inc(Z["s_gs"], 16)

            gates(0)
            with sp.Fori(1, NT) as t:
                gates(t)
            chunk(N_A, 0, wbh[:, :, 0:P], wbp[:, :, 0:P])
            chunk(N_A + 1, 1, wbh[:, :, P:2 * P], wbp[:, :, P:2 * P])
            sp.wait_ge(Z["s_ol"], NT)
            sp.wait_ge(Z["s_o"], NT)
            sp.dma_start(mixr[:], spill[0:4].rearrange("h p n -> p h n")).then_inc(Z["s_mixr"], 16)
            sp.wait_ge(Z["s_gst0"], 16 * 12)
            sp.wait_ge(Z["s_gst1"], 16 * 12)

            def branch(m, more):
                for b in range(2):
                    sp.wait_ge(Z["s_free"], 2 * m + (N_A + 2 * b - 2))
                    sp.dma_start(ghg[:, b], one(spill[bass.ds(m + (8 + b), 1)])).then_inc(Z[f"s_gl{b}"], 16)
                    sp.dma_start(gpl[:, b], one(spill[bass.ds(m + (16 + b), 1)])).then_inc(Z[f"s_gl{b}"], 16)
                    if more:
                        at_ = bass.ts(m + (b + 2), P)
                        chunk(m + (N_A + b + 2), b, wbh[:, :, at_], wbp[:, :, at_])

            with sp.Fori(0, KC // 2 - 1) as pair:
                branch(pair * 2, True)
            branch(KC - 2, False)
            rawrow = raw[:].rearrange("p s k n -> p s (k n)")
            for k in range(KC):
                sp.wait_ge(Z["s_lo"], N_CH + k - 1)
                sp.dma_start(rawrow[:, k % 2, 0:HALF], wov[k, :, 0:HALF]).then_inc(Z[f"s_raw{k % 2}"], 16)
                sp.dma_start(rawrow[:, k % 2, HALF:D], wov[k, :, HALF:D]).then_inc(Z[f"s_raw{k % 2}"], 16)
            sp.wait_ge(Z["s_mm"], N_CH)
            sp.wait_ge(Z["s_hn"], 16 + 2 * KC)
            order = [(0, 0, 2 * D, g_post_mix), (2, 2, 3 * D, None), (1, 4, 4 * D, g_pre_ffn), (3, 6, 5 * D, g_post_ffn)]
            for n, (r, piece, off, gain) in enumerate(order):
                sp.wait_ge(Z["s_rows"], n)
                sp.dma_start(rows[:, r], ada_d[piece:piece + 2, :].rearrange("a n -> (a n)").partition_broadcast(P)).then_inc(Z["s_rowl"], 16)
                sp.dma_start(rtmp[:, 0], b_ada[0, off:off + D].partition_broadcast(P)).then_inc(Z["s_rowl"], 16)
                sp.dma_start(rtmp[:, 1], (gain if gain is not None else b_ada[:, off:off + D])[0].partition_broadcast(P)).then_inc(Z["s_rowl"], 16)
            sp.wait_ge(Z["s_rows"], 4)
            sp.dma_start(wr[:, :, 0:G], w_rg[0].rearrange("(k p) n -> p k n", p=P)).then_inc(Z["s_wr"], 16)
            sp.dma_start(wr[:, :, G:G + E], w_re[0].rearrange("(k p) n -> p k n", p=P)).then_inc(Z["s_wr"], 16)
            sp.dma_start(brow[:, 0:G], b_rg[0].partition_broadcast(P)).then_inc(Z["s_wr"], 16)
            sp.dma_start(brow[:, G:G + E], b_re[0].partition_broadcast(P)).then_inc(Z["s_wr"], 16)
            for t in range(2):
                sp.dma_start(xr[:, t], xv[t]).then_inc(Z[f"s_xr{t}"], 16)
            for t in range(NT):
                b = t % 2
                sp.wait_ge(Z["s_h"], t + 1)
                sp.dma_start(h_d[t * P:(t + 1) * P, :], hh[:, b]).then_inc(Z[f"s_hst{b}"], 16)
                if t + 2 < NT:
                    sp.dma_start(xr[:, b], xv[t + 2]).then_inc(Z[f"s_xr{b}"], 16)
                sp.wait_ge(Z["s_hn2"], t + 1)
                sp.dma_start(hn2_d[t * P:(t + 1) * P, :], hn2[:, b]).then_inc(Z[f"s_nst{b}"], 16)

            def piece(src, slot):
                sp.dma_start(raw6[:, slot] if src.shape[1] == 4 else raw6[:, slot].rearrange("p k n -> p (k n)").rearrange("p (k n) -> p k n", k=2),
                             src).then_inc(s_r6[slot], 16)

            def gate_up(e):
                for k in (0, 4):
                    yield egv[e, :, k:k + 4, :] if isinstance(e, int) else egv[bass.ds(e, 1), :, k:k + 4, :].rearrange("a p k n -> (a p) k n")
                    yield euv[e, :, k:k + 4, :] if isinstance(e, int) else euv[bass.ds(e, 1), :, k:k + 4, :].rearrange("a p k n -> (a p) k n")

            def down(e):
                for k in (0, 2):
                    yield edv[e, :, k:k + 2, :] if isinstance(e, int) else edv[bass.ds(e, 1), :, k:k + 2, :].rearrange("a p k n -> (a p) k n")

            sp.wait_ge(Z["s_wo"], NT)
            for n, src in enumerate(gate_up(0)):
                piece(src, n)
            for n, src in enumerate([*gate_up(1)][0:2]):
                piece(src, 4 + n)
            with sp.Fori(0, E // 2 - 1) as i:
                gu = [[*gate_up(i * 2 + k)] for k in (1, 2, 3)]
                for j, src in enumerate([*gu[0][2:4], *down(i * 2), *gu[1], *down(i * 2 + 1), *gu[2][0:2]]):
                    sp.wait_ge(Z["s_plo"], i * 12 + (j + 1))
                    settle(sp)
                    piece(src, j % 6)
            n = 6 * (E - 1)
            for src in [*[*gate_up(E - 1)][2:4], *down(E - 2), *down(E - 1)]:
                sp.wait_ge(Z["s_plo"], n - 5)
                piece(src, n % 6)
                n += 1
            assert n == 6 * E
            sp.wait_ge(Z["s_tabd"], 2)
            nov = sp.value_load(ovt[0:1, 0:1], min_val=0, max_val=NOV)
            with sp.If(nov > 0):
                with sp.Fori(0, NOV) as j:
                    with sp.If(nov > j):
                        e = sp.value_load(ovt[0:1, bass.ds(j + 1, 1)], min_val=0, max_val=E - 1)
                        for k, src in enumerate([*gate_up(e), *down(e)]):
                            sp.wait_ge(Z["s_plo"], j * 6 + (6 * E + k - 5))
                            piece(src, k)
            for t in range(NT):
                b = t % 2
                if t >= 2:
                    sp.wait_ge(Z["s_fin"], t - 1)
                if t == 0:
                    sp.wait_ge(Z["s_ovd"], 1)
                sp.dma_start(hb[:, b], h_d[t * P:(t + 1) * P, :]).then_inc(Z[f"s_hb{b}"], 16)
                if t >= 1:
                    sp.wait_ge(Z["s_fin"], t)
                    sp.dma_start(outv[t - 1], yo[:, (t - 1) % 2]).then_inc(Z[f"s_out{(t - 1) % 2}"], 16)
            sp.wait_ge(Z["s_fin"], NT)
            sp.dma_start(outv[NT - 1], yo[:, (NT - 1) % 2]).then_inc(Z[f"s_out{(NT - 1) % 2}"], 16)
            sp.wait_ge(Z["s_out0"], 16 * 4)
            sp.wait_ge(Z["s_out1"], 16 * 4)

        @block.scalar
        def _(act):
            own = Chain(act, Z["s_act"])

            def do(out_, in_, f, **kw):
                return nc.scalar.activation(out_, in_, f, **kw)

            eps = small[:, 0:1]
            for t in range(NT):
                act.dma_start(xt[:, t], xv[t]).then_inc(Z["s_x"], 16)
            act.wait_ge(Z["s_cols"], 1)
            do(small[:, 8:16], cols[:, C_COND:C_COND + 8], ACT.Silu).then_inc(Z["s_cond"], 1)
            act.wait_ge(Z["s_x"], 16 * NT)
            act.wait_ge(Z["s_const"], 1)
            for t in range(NT):
                if t:
                    act.wait_ge(Z["s_ssq"], t)
                do(win2[:], xt[:, t], ACT.Square, accum_out=small[:, 16 + t:17 + t]).then_inc(Z["s_ssq"], 1)
            act.wait_ge(Z["s_ssq"], NT)
            do(small[:, 24:32], small[:, 16:24], ACT.Sqrt, scale=1.0 / D, bias=eps).then_inc(Z["s_sd"], 1)
            act.wait_ge(Z["s_lbx"], 1)
            do(small[:, 40:48], small[:, 40:48], ACT.Exp).then_inc(Z["s_lbx"], 1)
            for n in range(16):
                hf, k = divmod(n, KC)
                act.wait_ge(Z["s_val"], n + 1)
                do(hnh[:, k, bass.ts(hf, HALF)], valr[:, n % 2], ACT.Copy).then_inc(Z["s_hh"], 1)

            def round_chunk(cn, slot, per_slot):
                act.wait_ge(Z[f"s_raw{slot}"], 32 * per_slot)
                if not (isinstance(cn, int) and cn < 2):
                    act.wait_ge(Z["s_mm"], cn - 1)
                do(wh[:, slot], raw[:, slot], ACT.Copy).then_inc(Z["s_hi"], 1)

            round_chunk(0, 0, 1)
            round_chunk(1, 1, 1)

            def evac(cn, slot, dst, f, **kw):
                act.wait_ge(Z["s_mm"], cn + 1)
                do(dst[:, 0:HALF], A[2 * slot][:, :], f, **kw)
                return do(dst[:, HALF:S], A[2 * slot + 1][:, :], f, **kw)

            def row_copy(p):
                act.wait_ge(Z["s_adam"], p + 1)
                if p:
                    act.wait_ge(Z["s_rowst"], 16 * p)
                do(rowr[:], A[6][0:1, :], ACT.Copy).then_inc(Z["s_rowc"], 1)
                act.wait_ge(Z["s_rowc"], p + 1)
                act.dma_start(ada_d[p:p + 1, :], rowr[:]).then_inc(Z["s_rowst"], 16)

            for cn in range(12):
                kind, j = divmod(cn, 4)
                evac(cn, cn % 2, (Bc, vT, ub)[kind][:, j], ACT.Sigmoid if kind == 0 else ACT.Copy).then_inc(Z["s_free"], 1)
                if cn < 8:
                    row_copy(cn)
                round_chunk(cn + 2, cn % 2, cn // 2 + 2)
            act.wait_ge(Z["s_B"], 1)
            for j in range(H):
                do(Bc[:, j], Bc[:, j], ACT.Ln).then_inc(Z["s_ln"], 1)
            act.wait_ge(Z["s_acc"], 12)
            with act.Fori(0, 4 // 2) as pair:
                j = pair * 2
                for b in range(2):
                    evac(j + (12 + b), b, Qq[:, bass.ds(j + b, 1)].rearrange("p a n -> p (a n)"), ACT.Silu).then_inc(Z["s_free"], 1)
                    act.wait_ge(Z[f"s_raw{b}"], 32 * 8 + 16 * j)
                    act.wait_ge(Z["s_mm"], j + (13 + b))
                    do(wh[:, b], raw[:, b], ACT.Copy).then_inc(Z["s_hi"], 1)
            for t in range(NT):
                act.wait_ge(Z["s_vt"], t + 1)
                do(Vv[:, t], A[6 + t % 2][:, :], ACT.Copy).then_inc(Z["s_ve"], 1)
            for n in range(8):
                g, hf = divmod(n, 2)
                act.wait_ge(Z["s_pm"], n + 1)
                if n == 0:
                    act.wait_ge(Z["s_pm"], 8)
                if n >= 4 and hf == 0:
                    act.wait_ge(Z[f"s_gst{g % 2}"], 16)
                do(gt[:, g % 2, bass.ts(hf, HALF)], A[(4, 5, 6, 7, 0, 1, 2, 3)[n]][:, :], ACT.Copy,
                   scale=cols[:, C_PS + g:C_PS + g + 1]).then_inc(Z["s_pe"], 1)
                if hf:
                    act.wait_ge(Z["s_pe"], n + 1)
                    act.dma_start(spill[g], gt[:, g % 2]).then_inc(Z[f"s_gst{g % 2}"], 16)
            for j in range(4):
                cn, b = 16 + j, j % 2
                act.wait_ge(Z[f"s_gst{b}"], 16 * (2 + j // 2))
                act.wait_ge(Z["s_mm"], cn + 1)
                do(gt[:, b, 0:HALF], A[2 * b][:, :], ACT.Silu)
                do(gt[:, b, HALF:S], A[2 * b + 1][:, :], ACT.Silu).then_inc(Z["s_free"], 1)
                act.wait_ge(Z["s_free"], cn + 1)
                own.link(do(gt[:, b], gt[:, b], ACT.Copy, scale=cols[:, C_NG + j:C_NG + j + 1]))
                act.dma_start(spill[4 + j], gt[:, b]).then_inc(Z[f"s_gst{b}"], 16)
                round_chunk(cn + 2, b, cn // 2 + 2)

            def gate_evac(t, b):
                act.wait_ge(Z[f"s_gst{b}"], 16 * t + 64)
                act.wait_ge(Z["s_mm"], 2 * t + (N_IN + 1 + b))
                do(gt[:, b, 0:HALF], A[2 * b][:, :], ACT.Copy)
                do(gt[:, b, HALF:S], A[2 * b + 1][:, :], ACT.Copy).then_inc(Z["s_free"], 1)
                act.wait_ge(Z["s_free"], 2 * t + (N_IN + 1 + b))
                act.dma_start(spill[bass.ds(2 * t + (8 + b), 1)].rearrange("a p n -> p (a n)"), gt[:, b]).then_inc(Z[f"s_gst{b}"], 16)
                act.wait_ge(Z[f"s_raw{b}"], 32 * 12 + 32 * t)
                do(wh[:, b], raw[:, b], ACT.Copy).then_inc(Z["s_hi"], 1)

            def squares(t):
                act.wait_ge(Z["s_o"], t + 1)
                past(act, Z["s_osq"], t)
                for h in range(H):
                    last = do(sqs[:, h], A[6][:, h * P:(h + 1) * P], ACT.Square, accum_out=small[:, 64 + h:65 + h])
                last.then_inc(Z["s_osq"], 1)
                act.wait_ge(Z["s_osq"], t + 1)
                do(small[:, 68:72], small[:, 64:68], ACT.Sqrt, scale=1.0 / P, bias=eps).then_inc(Z["s_osd"], 1)

            def o_high(t):
                act.wait_ge(Z["s_oval"], t + 1)
                settle(act)
                do(oh[:, :, bass.ts(t, P)], ov[:], ACT.Copy).then_inc(Z["s_oh"], 1)

            def tile(t, last_tile):
                tok = bass.ts(t, P)
                do(E0[:], Bc[:, :, tok], ACT.Exp).then_inc(Z["s_E"], 1)
                do(Kc[:], Kk[:, :, tok], ACT.Copy).then_inc(Z["s_kc"], 1)

                def factor(k):
                    act.wait_ge(Z["s_D"], 8 * t + (k + 1))
                    if k == 2:
                        act.wait_ge(Z["s_kd"], t + 1)
                    elif k > 2:
                        act.wait_ge(Z["s_QK"], 7 * t + (k - 2))
                    do(Ee[:, k % 2], Dd[:, k % 2], ACT.Exp).then_inc(Z["s_E"], 1)

                factor(0)
                factor(1)
                if last_tile is not None:
                    squares(last_tile)
                factor(2)
                act.wait_ge(Z["s_kt"], t + 1)
                do(kdN[:], A[7][:, :].rearrange("p (h n) -> p h n", h=H), ACT.Copy).then_inc(Z["s_kn"], 1)
                factor(3)
                factor(4)
                if last_tile is not None:
                    o_high(last_tile)
                    gate_evac(last_tile, 1)
                for k in range(5, 8):
                    factor(k)
                gate_evac(t, 0)

            act.wait_ge(Z["s_mask"], 1)
            tile(0, None)
            with act.Fori(1, NT) as t:
                tile(t, t - 1)
            squares(NT - 1)
            o_high(NT - 1)
            gate_evac(NT - 1, 1)

            act.wait_ge(Z["s_mixr"], 16)
            for g in range(H):
                do(mh[:, g], mixr[:, g], ACT.Copy).then_inc(Z["s_mh"], 1)

            biasc = small[:, 4:8].rearrange("p (a b) -> p a b", a=2)

            def branch(m, more):
                past(act, Z["s_sg"], m)
                for a in range(2):
                    own.link(do(biasc[:, a], cols[:, bass.ds(m + (C_BGATE + 8 * a), 2)], ACT.Copy))
                for b in range(2):
                    act.wait_ge(Z[f"s_gl{b}"], 16 * m + 32)
                    do(ghg[:, b], ghg[:, b], ACT.Sigmoid, bias=biasc[:, 0, b:b + 1])
                    do(gpl[:, b], gpl[:, b], ACT.Sigmoid, bias=biasc[:, 1, b:b + 1]).then_inc(Z["s_sg"], 1)
                for b in range(2):
                    for hf in range(2):
                        act.wait_ge(Z["s_bval"], 2 * m + (2 * b + hf + 1))
                        do(hnh[:, bass.ds(m + b, 1), bass.ts(hf, HALF)].rearrange("p a n -> p (a n)"), valr[:, hf], ACT.Copy).then_inc(Z["s_mTh"], 1)
                    if more:
                        act.wait_ge(Z[f"s_raw{b}"], 16 * m + 32 * 20)
                        act.wait_ge(Z["s_mm"], m + (N_A + 1 + b))
                        do(wh[:, b], raw[:, b], ACT.Copy).then_inc(Z["s_hi"], 1)

            branch(0, True)
            with act.Fori(1, KC // 2 - 1) as pair:
                own.enter(pair, 2, 1)
                branch(pair * 2, True)
            own.leave(KC // 2 - 1)
            branch(KC - 2, False)
            act.wait_ge(Z["s_mm"], N_CH)
            for k in range(KC):
                act.wait_ge(Z[f"s_raw{k % 2}"], 32 * (23 + k // 2))
                do(woh[:, k], raw[:, k % 2].rearrange("p k n -> p (k n)"), ACT.Copy).then_inc(Z["s_hi"], 1)

            def turned(t):
                for q in range(2):
                    act.wait_ge(Z["s_h2T"], 2 * t + q + 1)
                    if q == 0 and t:
                        act.wait_ge(Z["s_rt"], t)
                    do(h2T[:, 4 * q:4 * q + 4].rearrange("p k n -> p (k n)"), A[4 + q][:, :], ACT.Copy).then_inc(Z["s_h2e"], 1)

            for t in range(NT):
                b = t % 2
                pr = [A[2 * b], A[2 * b + 1]]
                act.wait_ge(Z["s_wo"], t + 1)
                if t == 0:
                    act.wait_ge(Z["s_rows"], 4)
                for q in range(2):
                    last = do(junk[:, bass.ts(q, HALF)], pr[q][:, :], ACT.Square, accum_out=small[:, 80 + q:81 + q])
                last.then_inc(Z["s_mixsq"], 1)
                act.wait_ge(Z["s_mixsd"], t + 1)
                do(small[:, 83:84], small[:, 82:83], ACT.Sqrt, scale=1.0 / D, bias=eps).then_inc(Z["s_mt"], 1)
                if t:
                    turned(t - 1)
                act.wait_ge(Z["s_h"], t + 1)
                do(junk[:], hh[:, b], ACT.Square, accum_out=small[:, 88:89]).then_inc(Z["s_hsq"], 1)
                act.wait_ge(Z["s_hsq"], t + 1)
                do(small[:, 89:90], small[:, 88:89], ACT.Sqrt, scale=1.0 / D, bias=eps).then_inc(Z["s_hsd"], 1)
            turned(NT - 1)

            act.wait_ge(Z["s_ge"], 1)
            do(R[0][:, :, :, 0], R[0][:, :, :, 0], ACT.Exp).then_inc(Z["s_ge"], 1)
            act.wait_ge(Z["s_ge"], 3)
            do(R[2][:, :, 0], R[2][:, :, 0], ACT.Exp).then_inc(Z["s_ge"], 1)

            def hi(turn, slot, free):
                act.wait_ge(s_r6[slot], 16 * turn)
                if free is not None:
                    act.wait_ge(Z["s_pc"], free)
                do(eh[:, slot], raw6[:, slot], ACT.Copy).then_inc(Z["s_phi"], 1)

            def x_high(cnt, b, q):
                act.wait_ge(Z["s_xTp"], 2 * cnt + (q + 1))
                do(xTh[:, b, 4 * q:4 * q + 4].rearrange("p k n -> p (k n)"), A[4][:, :], ACT.Copy).then_inc(Z["s_xTh"], 1)

            def silu(e, b, done):
                act.wait_ge(Z["s_pc"], done)
                if not (isinstance(e, int) and e == 0):
                    act.wait_ge(Z["s_a"], e)
                do(sil[:], A[2 * b][:, :], ACT.Silu).then_inc(Z["s_sil"], 1)

            def a_high(e, b):
                act.wait_ge(Z["s_aT"], e + 1)
                do(aTh[:, b].rearrange("p k n -> p (k n)"), A[5][:, :], ACT.Copy).then_inc(Z["s_aTh"], 1)

            def y_store(e, row, done):
                act.wait_ge(Z["s_pc"], done)
                if not (isinstance(e, int) and e == 0):
                    act.wait_ge(Z["s_yst"], 16 * e)
                do(yy[:, 0:HALF], A[6][:, :], ACT.Copy)
                do(yy[:, HALF:D], A[7][:, :], ACT.Copy).then_inc(Z["s_ycp"], 1)
                act.wait_ge(Z["s_ycp"], e + 1)
                act.dma_start(y_d[row, :], yy[0:BLK, :]).then_inc(Z["s_yst"], 16)

            act.wait_ge(Z["s_rt"], NT)
            for n in range(6):
                hi(1, n, None)
            for e in range(2):
                for q in range(2):
                    x_high(e, e, q)

            def step(e, i, b, first=False, last_x=False):
                n0 = 4 + 6 * (1 - b)

                def h(j):
                    k = n0 + j
                    hi(2 * i + (k // 6 + 1), k % 6, i * 12 + (k - 5))
                silu(e - 1, 1 - b, 4 if first else i * 12 + (n0 - 2))
                h(2)
                h(3)
                if not first:
                    y_store(e - 2, bass.ts(e - 2, BLK), i * 12 + n0)
                if not last_x:
                    x_high(e + 1, 1 - b, 0)
                h(4)
                h(5)
                a_high(e - 1, 1 - b)
                if not last_x:
                    x_high(e + 1, 1 - b, 1)
                h(6)
                h(7)

            step(1, 0, 1, first=True)
            step(2, 0, 0)
            with act.Fori(1, E // 2 - 1) as i:
                step(i * 2 + 1, i, 1)
                step(i * 2 + 2, i, 0)
            step(E - 1, E // 2 - 1, 1, last_x=True)
            silu(E - 1, 1, 6 * E - 4)
            a_high(E - 1, 1)
            y_store(E - 2, bass.ts(E - 2, BLK), 6 * E - 2)
            y_store(E - 1, bass.ts(E - 1, BLK), 6 * E)
            act.wait_ge(Z["s_tabd"], 2)
            nov = act.value_load(ovt[0:1, 0:1], min_val=0, max_val=NOV)
            with act.If(nov > 0):
                with act.Fori(0, NOV) as j:
                    with act.If(nov > j):
                        for q in range(2):
                            x_high(j + E, 0, q)
                        for k in range(6):
                            hi(j + (E + 1), k, j * 6 + (6 * E + k - 5))
                        silu(j + E, 0, j * 6 + (6 * E + 4))
                        a_high(j + E, 0)
                        y_store(j + E, bass.ts(j + E, BLK), j * 6 + (6 * E + 6))
                    with act.If(nov < j + 1):
                        act.dma_start(y_d[bass.ts(j + E, BLK), :], yy[0:BLK, :]).then_inc(Z["s_yst"], 16)
                    act.wait_ge(Z["s_yst"], 16 * j + 16 * (E + 1))
                    settle(act)
            act.wait_ge(Z["s_yst"], 16 * E)
            do(small[:, 121:122], small[:, 0:1], ACT.Copy).then_inc(Z["s_ovd"], 1)
            for t in range(NT):
                b = t % 2
                act.wait_ge(Z["s_ysum"], t + 1)
                do(ysq[:], yo[:, b], ACT.Square, accum_out=small[:, 96 + b:97 + b]).then_inc(Z["s_ysq"], 1)
                act.wait_ge(Z["s_ysq"], t + 1)
                do(small[:, 98 + b:99 + b], small[:, 96 + b:97 + b], ACT.Sqrt, scale=1.0 / D, bias=eps).then_inc(Z["s_ysd"], 1)

        @block.tensor
        def _(pe):
            def mm(dst, l, r, start, stop, **kw):
                return nc.tensor.matmul(dst, l, r, start=start, stop=stop, **kw)

            pe.wait_ge(Z["s_ident"], 2)
            pe.wait_ge(Z["s_vec"], 16 * 7)
            nc.tensor.transpose(A[7][:, 0:N_VEC], vecs[:, :], ident[0:N_VEC, 0:N_VEC]).then_inc(Z["s_vecT"], 1)
            pe.wait_ge(Z["s_acc"], 4)
            pe.wait_ge(Z["s_ones"], 1)
            for j in range(16):
                last = mm(A[6][:, j:j + 1], acc0[:, j // 4, (j % 4) * P:(j % 4 + 1) * P], ones[:, 0:1], True, True)
            last.then_inc(Z["s_mod"], 1)
            pe.wait_ge(Z["s_xs"], NT)
            for n in range(16):
                hf, k = divmod(n, KC)
                if n >= 4:
                    pe.wait_ge(Z["s_val"], n - 3)
                for q in range(4):
                    last = nc.tensor.transpose(A[n % 4][:, q * P:(q + 1) * P], xt[:, 4 * hf + q, k * P:(k + 1) * P], ident[:, :])
                last.then_inc(Z["s_xT"], 1)

            def chunk_groups(cn, slot, free):
                pe.wait_ge(Z["s_lo"], cn + 1)
                if free is not None:
                    pe.wait_ge(Z["s_free"], free)
                for hf in range(2):
                    dst = A[2 * slot + hf][:, :]
                    todo = [(l, r, k) for k in range(KC) for l, r in ((wh, hnh), (wh, hnl), (wl, hnh))]
                    for g in range(3):
                        for n, (l, r, k) in enumerate(todo[8 * g:8 * g + 8]):
                            last = mm(dst, l[:, slot, k, :], r[:, k, hf * HALF:(hf + 1) * HALF],
                                      g == 0 and n == 0, g == 2 and n == 7)
                        if hf == 1 and g == 2:
                            last.then_inc(Z["s_mm"], 1)
                        yield

            def chunk(cn, slot, free):
                for _ in chunk_groups(cn, slot, free):
                    pass

            pe.wait_ge(Z["s_hn"], 16)
            pe.wait_ge(Z["s_val"], 16)
            for cn in range(8):
                chunk(cn, cn % 2, cn - 1 if cn >= 2 else None)
                pe.wait_ge(Z["s_acc"], 5 + cn)
                if cn:
                    pe.wait_ge(Z["s_rowc"], cn)
                else:
                    pe.wait_ge(Z["s_modc"], 1)
                mm(A[6][0:1, :], ones[:, 0:1], acc1[:, cn % 2, :], True, True).then_inc(Z["s_adam"], 1)
            with pe.Fori(8 // 2, 16 // 2) as pair:
                cn = pair * 2
                for b in range(2):
                    chunk(cn + b, b, cn + (b - 1))
            pe.wait_ge(Z["s_rowc"], 8)
            for t in range(NT):
                if t >= 2:
                    pe.wait_ge(Z["s_ve"], t - 1)
                for h in range(H):
                    last = nc.tensor.transpose(A[6 + t % 2][:, h * P:(h + 1) * P], vT[:, h, t * P:(t + 1) * P], ident[:, :])
                last.then_inc(Z["s_vt"], 1)
            pe.wait_ge(Z["s_pw"], 16)
            pe.wait_ge(Z["s_ve"], NT)
            pe.wait_ge(Z["s_free"], 16)
            for n in range(8):
                g, hf = divmod(n, 2)
                pe.wait_ge(Z["s_pool"], g + 1)
                mm(A[(4, 5, 6, 7, 0, 1, 2, 3)[n]][:, :], poolw[:, g, :], ub[:, g, hf * HALF:(hf + 1) * HALF], True, True).then_inc(Z["s_pm"], 1)
            pe.wait_ge(Z["s_pe"], 8)
            for cn in range(16, 20):
                chunk(cn, cn % 2, cn - 1)

            pe.wait_ge(Z["s_mask"], 1)

            def v_of(t, h):
                return Vv[:, bass.ds(t, 1), h * P:(h + 1) * P].rearrange("p a n -> p (a n)")

            def turn_o(t):
                pe.wait_ge(Z["s_on"], t + 1)
                for h in range(H):
                    last = nc.tensor.transpose(A[7][:, h * P:(h + 1) * P], on[:, h], ident[:, :])
                last.then_inc(Z["s_ot"], 1)

            def tile(t, last_tile):
                tok = bass.ts(t, P)

                def diag():
                    pe.wait_ge(Z["s_kc"], t + 1)
                    past(pe, Z["s_mg"], 8 * t)
                    for h in range(H):
                        last = mm(A[4][:, h * P:(h + 1) * P], Kc[:, h], Qq[:, h, tok], True, True)
                    last.then_inc(Z["s_sc"], 1)

                def turn_k():
                    pe.wait_ge(Z["s_kd"], t + 1)
                    past(pe, Z["s_S"], t)
                    for h in range(H):
                        last = nc.tensor.transpose(A[7][:, h * P:(h + 1) * P], kd[:, h], ident[:, :])
                    last.then_inc(Z["s_kt"], 1)

                def level(k):
                    def go():
                        pe.wait_ge(Z["s_QK"], 7 * t + k)
                        past(pe, Z["s_mg"], 8 * t + (k - 1))
                        for h in range(H):
                            last = mm(A[4 + k % 2][:, h * 64:(h + 1) * 64], KL[:, k % 2, h], QL[:, k % 2, h], True, True)
                        last.then_inc(Z["s_sc"], 1)
                    return go

                def turn_last():
                    if last_tile is not None:
                        pe.wait_ge(Z["s_kn"], t + 1)
                        turn_o(last_tile)

                def outputs():
                    pe.wait_ge(Z["s_mg"], 8 * t + 8)
                    past(pe, Z["s_S"], t)
                    past(pe, Z["s_on"], t)
                    pe.wait_ge(Z["s_qe"], t + 1)
                    for h in range(H):
                        mm(A[6][:, h * P:(h + 1) * P], Sc[:, h], v_of(t, h), True, False)
                        last = mm(A[6][:, h * P:(h + 1) * P], qe[:, h], St[:, h], False, True)
                    last.then_inc(Z["s_o"], 1)
                    pe.wait_ge(Z["s_kn"], t + 1)
                    past(pe, Z["s_oval"], t)
                    for h in range(H):
                        last = mm(A[7][:, h * P:(h + 1) * P], kdN[:, h], v_of(t, h), True, True)
                    last.then_inc(Z["s_st"], 1)

                steps = [diag, turn_k, level(1), level(2), turn_last] + [level(k) for k in range(3, 8)] + [None, outputs]
                n = 0
                for b in range(2):
                    for _ in chunk_groups(2 * t + (N_IN + b), b, 2 * t + (N_IN + b - 1)):
                        if steps[n]:
                            steps[n]()
                        n += 1
                assert n == len(steps)

            tile(0, None)
            with pe.Fori(1, NT) as t:
                tile(t, t - 1)
            turn_o(NT - 1)

            pe.wait_ge(Z["s_oh"], NT)
            pe.wait_ge(Z["s_ol"], NT)
            pe.wait_ge(Z["s_ml"], H)
            pe.wait_ge(Z["s_free"], N_A)
            with pe.Fori(0, KC // 2) as pair:
                m = pair * 2
                for b in range(2):
                    pe.wait_ge(Z["s_lo"], m + (N_A + b + 1))
                    for hf in range(2):
                        pe.wait_ge(Z["s_free"], 2 * m + (N_A + 2 * b + hf - 1))
                        cols_ = slice(hf * HALF, (hf + 1) * HALF)
                        for br, (vh, vl) in enumerate(((oh, ol), (mh, ml))):
                            todo = [(l, r, k) for k in range(H) for l, r in ((wh, vh), (wh, vl), (wl, vh))]
                            for n, (l, r, k) in enumerate(todo):
                                last = mm(A[2 * hf + br][:, :], l[:, b, 4 * br + k, :], r[:, k, cols_], n == 0, n == 11)
                        last.then_inc(Z["s_mm" if hf else "s_br"], 1)

            pe.wait_ge(Z["s_lo"], N_CH + KC)
            pe.wait_ge(Z["s_hn"], 16 + 2 * KC)
            pe.wait_ge(Z["s_free"], N_A + 2 * KC)

            def project(t):
                if t >= 2:
                    pe.wait_ge(Z["s_hsq"], t - 1)
                tk = slice(t * P, (t + 1) * P)
                for q in range(2):
                    n = 0
                    for k in range(KC):
                        for l, r in ((hnh, woh), (hnh, wol), (hnl, woh)):
                            last = mm(A[2 * (t % 2) + q][:, :], l[:, k, tk], r[:, k, q * HALF:(q + 1) * HALF], n == 0, n == 23)
                            n += 1
                last.then_inc(Z["s_wo"], 1)

            def route(t):
                pe.wait_ge(Z["s_hn2"], t + 1)
                for q in range(2):
                    if t:
                        pe.wait_ge(Z["s_h2e"], 2 * t - 1 + q)
                    for k in range(4):
                        last = nc.tensor.transpose(A[4 + q][:, k * P:(k + 1) * P], hn2[:, t % 2, (4 * q + k) * P:(4 * q + k + 1) * P], ident[:, :])
                    last.then_inc(Z["s_h2T"], 1)
                pe.wait_ge(Z["s_h2e"], 2 * t + 2)
                pe.wait_ge(Z["s_wr"], 64)
                if t:
                    pe.wait_ge(Z["s_L"], t)
                for k in range(KC):
                    last = mm(A[6][:, 0:G + E], h2T[:, k, :], wr[:, k, :], k == 0, k == KC - 1)
                last.then_inc(Z["s_rt"], 1)

            for t in range(NT):
                project(t)
                if t:
                    route(t - 1)
            route(NT - 1)

            pe.wait_ge(Z["s_M"], 1)
            Mv = R[7][:].rearrange("p t g e -> p t (g e)")
            pos = A[0][:, 0:NT * E].rearrange("p (t e) -> p t e", e=E)
            pe.wait_ge(Z["s_iota"], 1)
            mm(pos, tri[:], Mv, True, False, skip_group_check=True)
            for s in range(NT - 1):
                last = mm(pos[:, s + 1:, :], ones[:], Mv[:, s:s + 1, :].to_broadcast([P, NT - 1 - s, E]), False, s == NT - 2,
                          skip_group_check=True)
            mm(A[1][:, 0:E], ones[:], c32[:, 0, :], True, True).then_inc(Z["s_pos"], 1)
            for n in range(2 * NT):
                pe.wait_ge(Z["s_AB"], n + 1)
                mm(A[2][0:BLK, 0:NCOL], Aoh[:, n % 2, 0:BLK], Boh[:, n % 2, 0:NCOL], n == 0, n == 2 * NT - 1).then_inc(Z["s_slots"], 1)

            def turn_x(cnt, b, q):
                if q == 0:
                    pe.wait_ge(Z[f"s_xg{b}"], cnt)
                for k in range(4):
                    last = nc.tensor.transpose(A[4][:, k * P:k * P + BLK], xg[0:BLK, b, (4 * q + k) * P:(4 * q + k + 1) * P], ident[0:BLK, 0:BLK])
                last.then_inc(Z["s_xTp"], 1)

            def gate_up_half(n, half, b, w):
                pe.wait_ge(Z["s_plo"], n + 2)
                g, u = A[2 * b][0:BLK, :], A[2 * b + 1][0:BLK, :]
                for k in range(4):
                    kk = 4 * half + k
                    st, sp_ = (kk == 0), (kk == KC - 1)
                    mm(g, xTh[:, b, kk, 0:BLK], eh[:, w[0], k, :], st, False)
                    mm(g, xTh[:, b, kk, 0:BLK], el[:, w[0], k, :], False, False)
                    mm(u, xTh[:, b, kk, 0:BLK], eh[:, w[1], k, :], st, False)
                    mm(u, xTh[:, b, kk, 0:BLK], el[:, w[1], k, :], False, False)
                    lg = mm(g, xTl[:, b, kk, 0:BLK], eh[:, w[0], k, :], False, sp_)
                    lu = mm(u, xTl[:, b, kk, 0:BLK], eh[:, w[1], k, :], False, sp_)
                lg.then_inc(Z["s_pc"], 1)
                lu.then_inc(Z["s_pc"], 1)
                return lu

            def turn_a(e, b):
                pe.wait_ge(Z["s_a"], e + 1)
                if not (isinstance(e, int) and e == 0):
                    pe.wait_ge(Z["s_aTl"], e)
                for k in range(4):
                    last = nc.tensor.transpose(A[5][:, k * P:k * P + BLK], aa[0:BLK, b, k * P:(k + 1) * P], ident[0:BLK, 0:BLK])
                last.then_inc(Z["s_aT"], 1)

            def down(e, n, b, w):
                pe.wait_ge(Z["s_aTl"], e + 1)
                if not (isinstance(e, int) and e == 0):
                    pe.wait_ge(Z["s_ycp"], e)
                for half in range(2):
                    pe.wait_ge(Z["s_plo"], n + (half + 1))
                    for kk in range(2):
                        k = 2 * half + kk
                        for q in range(2):
                            sl = (slice(None), w[half], 2 * kk + q)
                            mm(A[6 + q][0:BLK, :], aTh[:, b, k, 0:BLK], eh[sl], k == 0, False)
                            mm(A[6 + q][0:BLK, :], aTh[:, b, k, 0:BLK], el[sl], False, False)
                            last = mm(A[6 + q][0:BLK, :], aTl[:, b, k, 0:BLK], eh[sl], False, k == 3)
                    last.then_inc(Z["s_pc"], 1)
                return last

            def wait_x(cnt):
                pe.wait_ge(Z["s_xTl"], cnt)

            for e in range(2):
                for q in range(2):
                    if 2 * e + q:
                        wait_x(2 * e + q)
                    turn_x(16, e, q)
            wait_x(2)
            gate_up_half(0, 0, 0, (0, 1))
            gate_up_half(2, 1, 0, (2, 3))

            def pe_step(e, i, b, last_x=False):
                n0 = 4 + 6 * (1 - b)
                w = [(n0 + j) % 6 for j in range(6)]
                if not last_x:
                    wait_x(2 * e + 2)
                    turn_x(i * 16 + 32, 1 - b, 0)
                wait_x(2 * e + 2)
                gate_up_half(i * 12 + n0, 0, b, w[0:2])
                turn_a(e - 1, 1 - b)
                if not last_x:
                    wait_x(2 * e + 3)
                    turn_x(0, 1 - b, 1)
                gate_up_half(i * 12 + (n0 + 2), 1, b, w[2:4])
                down(e - 1, i * 12 + (n0 + 4), 1 - b, w[4:6])

            with pe.Fori(0, E // 2 - 1) as i:
                pe_step(i * 2 + 1, i, 1)
                pe_step(i * 2 + 2, i, 0)
            pe_step(E - 1, E // 2 - 1, 1, last_x=True)
            turn_a(E - 1, 1)
            n = 6 * E - 2
            down(E - 1, n, 1, (n % 6, (n + 1) % 6))
            pe.wait_ge(Z["s_tabd"], 2)
            nov = pe.value_load(ovt[0:1, 0:1], min_val=0, max_val=NOV)
            with pe.If(nov > 0):
                with pe.Fori(0, NOV) as j:
                    with pe.If(nov > j):
                        for q in range(2):
                            wait_x(j * 2 + (2 * E + q))
                            turn_x(16 * j + 16 * (E // 2 + 1), 0, q)
                        wait_x(j * 2 + (2 * E + 2))
                        pe.wait_ge(Z["s_aTl"], j + E)
                        gate_up_half(j * 6 + 6 * E, 0, 0, (0, 1))
                        gate_up_half(j * 6 + (6 * E + 2), 1, 0, (2, 3))
                        turn_a(j + E, 0)
                        down(j + E, j * 6 + (6 * E + 4), 0, (4, 5))

        @block.vector
        def _(dve):
            own = Chain(dve, Z["s_dve"])
            V = nc.vector
            V.memset(small[:, 0:1], EPS).then_inc(Z["s_const"], 1)
            V.memset(ones[:], 1.0).then_inc(Z["s_ones"], 1)
            dve.wait_ge(Z["s_iota"], 1)
            own.link(V.tensor_tensor(xorm[:], iS[:], iT[:], ALU.bitwise_xor))
            own.link(V.tensor_tensor(iS[:], iT[:], iS[:], ALU.is_gt))
            own.link(V.tensor_tensor(xorm[:], xorm[:], iS[:], ALU.mult))
            for n, h in enumerate(LEVELS):
                second = xorm[:].rearrange("p (n b) -> p n b", b=2 * h)[:, :, h:2 * h]
                mk = mask[:, n].rearrange("p (n b) -> p n b", b=h)
                t1 = mtmp[:].rearrange("p (n b) -> p n b", b=h)
                own.link(V.tensor_scalar(t1, second, float(h), None, ALU.is_ge))
                own.link(V.scalar_tensor_tensor(mk, second, float(2 * h), t1, ALU.is_lt, ALU.mult))
            dve.wait_ge(Z["s_vecT"], 1)
            V.tensor_copy(cols[:], A[7][:, 0:N_VEC]).then_inc(Z["s_cols"], 1)
            dve.wait_ge(Z["s_cols"], 1)
            l0, l1 = cols[:, C_LB0:C_LB0 + 4], cols[:, C_LB1:C_LB1 + 4]
            own.link(V.tensor_tensor(small[:, 32:36], l0, l1, ALU.max))
            V.tensor_tensor(small[:, 40:44], l0, small[:, 32:36], ALU.subtract)
            V.tensor_tensor(small[:, 44:48], l1, small[:, 32:36], ALU.subtract).then_inc(Z["s_lbx"], 1)

            dve.wait_ge(Z["s_cond"], 1)

            def ada_piece(dst, slot, turn):
                for k in range(8):
                    if k % 4 == 0:
                        dve.wait_ge(s_ada[slot + k // 4], 16 * turn)
                    src, sc_ = adab[:, slot + k // 4, k % 4, :], small[:, 8 + k:9 + k]
                    if k == 0:
                        own.link(V.tensor_scalar(dst, src, sc_, None, ALU.mult))
                    elif k < 7:
                        own.link(V.scalar_tensor_tensor(dst, src, sc_, dst, ALU.mult, ALU.add))
                    else:
                        V.scalar_tensor_tensor(dst, src, sc_, dst, ALU.mult, ALU.add).then_inc(Z["s_acc"], 1)

            ada_piece(acc0[:, 0], 0, 1)
            ada_piece(acc0[:, 1], 2, 1)
            dve.wait_ge(Z["s_sd"], 1)
            rs = small[:, 48:56]

            def rsqrt(dst, sd, ss, tmp, scale):
                own.link(V.reciprocal(dst, sd))
                own.link(V.tensor_scalar(tmp, ss, scale, EPS, ALU.mult, ALU.add))
                own.link(V.tensor_tensor(tmp, tmp, dst, ALU.mult))
                own.link(V.tensor_tensor(tmp, tmp, dst, ALU.mult))
                own.link(V.tensor_scalar(tmp, tmp, -0.5, 1.5, ALU.mult, ALU.add))
                own.link(V.tensor_tensor(dst, dst, tmp, ALU.mult))

            rsqrt(rs, small[:, 24:32], small[:, 16:24], small[:, 56:64], 1.0 / D)
            for t in range(NT):
                V.tensor_scalar(xt[:, t], xt[:, t], rs[:, t:t + 1], None, ALU.mult).then_inc(Z["s_xs"], 1)
            ada_piece(acc0[:, 2], 0, 2)
            ada_piece(acc0[:, 3], 2, 2)
            dve.wait_ge(Z["s_lbx"], 2)
            own.link(V.tensor_tensor(small[:, 32:36], small[:, 40:44], small[:, 44:48], ALU.add))
            own.link(V.reciprocal(small[:, 32:36], small[:, 32:36]))
            own.link(V.tensor_tensor(small[:, 32:36], small[:, 32:36], small[:, 40:44], ALU.mult))
            own.link(V.tensor_scalar(small[:, 36:40], small[:, 32:36], -1.0, 1.0, ALU.mult, ALU.add))
            dve.wait_ge(Z["s_mod"], 1)
            own.link(V.tensor_tensor(small[:, 72:80], A[6][:, 0:8], cols[:, C_BADA:C_BADA + 8], ALU.add))
            own.link(V.tensor_tensor(small[:, 104:112], A[6][:, 8:16], cols[:, C_BADA + 8:C_BADA + 16], ALU.add))
            V.scalar_tensor_tensor(small[:, 104:112], small[:, 104:112], 1.0, cols[:, C_GPRE:C_GPRE + 8], ALU.add, ALU.mult).then_inc(Z["s_modc"], 1)
            dve.wait_ge(Z["s_modc"], 1)
            dve.wait_ge(Z["s_ssq"], NT)
            for n in range(16):
                k = n % KC
                dve.wait_ge(Z["s_xT"], n + 1)
                if n >= 2:
                    dve.wait_ge(Z["s_hn"], n - 1)
                V.tensor_scalar(valr[:, n % 2], A[n % 4][:, :], small[:, 104 + k:105 + k], small[:, 72 + k:73 + k],
                                ALU.mult, ALU.add).then_inc(Z["s_val"], 1)

            def f_head(j):
                dve.wait_ge(Z["s_free"], j + 1)
                own.link(V.tensor_scalar(Bc[:, j], Bc[:, j], small[:, 36 + j:37 + j], small[:, 32 + j:33 + j], ALU.mult, ALU.add))
                return V.tensor_scalar(Kk[:, j], Bc[:, j], -1.0, 1.0, ALU.mult, ALU.add)

            for p in range(8):
                if p >= 2:
                    dve.wait_ge(Z["s_adam"], p - 1)
                ada_piece(acc1[:, p % 2], 2 * (p % 2), 3 + p // 2)
                if p < 4:
                    last = f_head(p)
                    if p == 3:
                        last.then_inc(Z["s_B"], 1)
            dve.wait_ge(Z["s_iota"], 1)
            own.link(V.tensor_scalar(small[:, 128:144], small[:, 128:144], 1.0, None, ALU.add))
            own.link(V.reciprocal(small[:, 128:144], small[:, 128:144]))
            own.link(V.memset(scanm[:], 1.0))
            own.link(V.memset(scanm[:].rearrange("p (t n) -> p t n", n=P)[:, :, 0:1], 0.0))
            dve.wait_ge(Z["s_hn"], 16)
            for g in range(H):
                dve.wait_ge(Z["s_free"], 9 + g)
                u = ub[:, g]
                src, w = u, 1
                for s in range(g + 1):
                    dst = (win1, win2)[s % 2][:]
                    V.tensor_copy(dst[:, 0:w], src[:, 0:w])
                    own.link(V.tensor_tensor(dst[:, w:S], src[:, w:S], src[:, 0:S - w], ALU.add))
                    src, w = dst, 2 * w
                own.link(V.tensor_tensor(src[:, 0:w], src[:, 0:w], small[:, 128:128 + w], ALU.mult))
                V.scalar_tensor_tensor(u[:, w:S], src[:, w:S], 1.0 / w, u[:, w:S], ALU.mult, ALU.subtract)
                V.tensor_tensor(u[:, 0:w], src[:, 0:w], u[:, 0:w], ALU.subtract).then_inc(Z["s_pool"], 1)
                dve.wait_ge(Z["s_pool"], g + 1)
            for j in range(H):
                dve.wait_ge(Z["s_ln"], j + 1)
                own.link(V.tensor_tensor_scan(Bc[:, j], scanm[:], Bc[:, j], 0.0, ALU.mult, ALU.add))
            dve.wait_ge(Z["s_vt"], NT)
            dve.wait_ge(Z["s_pm"], 8)
            own.link(V.memset(KL[:], 0.0))
            dve.wait_ge(Z["s_free"], 16)
            V.memset(St[:], 0.0).then_inc(Z["s_mask"], 1)
            dve.wait_ge(Z["s_mask"], 1)

            def state(t):
                dve.wait_ge(Z["s_o"], t + 1)
                dve.wait_ge(Z["s_st"], t + 1)
                dve.wait_ge(Z["s_ebl"], t + 1)
                for h in range(H):
                    last = V.scalar_tensor_tensor(St[:, h], St[:, h], small[:, 112 + h:113 + h], A[7][:, h * P:(h + 1) * P], ALU.mult, ALU.add)
                last.then_inc(Z["s_S"], 1)

            def normalise(t):
                dve.wait_ge(Z["s_osd"], t + 1)
                own.link(V.reciprocal(small[:, 116:120], small[:, 68:72]))
                V.tensor_tensor(on[:], A[6][:, :].rearrange("p (h n) -> p h n", h=H),
                                small[:, 116:120].unsqueeze(2).to_broadcast([P, H, P]), ALU.mult).then_inc(Z["s_on"], 1)

            def gate_o(t):
                dve.wait_ge(Z["s_ot"], t + 1)
                dve.wait_ge(Z["s_gs"], 16 * t + 16)
                past(dve, Z["s_oh"], t)
                V.tensor_tensor(ov[:], A[7][:, :].rearrange("p (h n) -> p h n", h=H), gs[:], ALU.mult).then_inc(Z["s_oval"], 1)

            def o_low(t):
                tok = bass.ts(t, P)
                dve.wait_ge(Z["s_oh"], t + 1)
                V.tensor_tensor(ol[:, :, tok], ov[:], oh[:, :, tok].bitcast(F32), ALU.subtract).then_inc(Z["s_ol"], 1)

            def tile(t, last_tile):
                tok = bass.ts(t, P)
                Bt, Kt, Qt = Bc[:, :, tok], Kk[:, :, tok], Qq[:, :, tok]

                def halves(v, h):
                    w = v.rearrange("p h (n b) -> p h n b", b=2 * h)
                    return w[:, :, :, 0:h], w[:, :, :, h:2 * h], w[:, :, :, h - 1:h].to_broadcast([P, H, 64 // h, h])

                def exponent(k):
                    if k == 0:
                        V.tensor_tensor(Dd[:, 0], Bt[:, :, P - 1:P].to_broadcast([P, H, P]), Bt, ALU.subtract).then_inc(Z["s_D"], 1)
                        return
                    h = LEVELS[k - 1]
                    b1, b2, ref = halves(Bt, h)
                    d1, d2, _ = halves(Dd[:, k % 2], h)
                    V.tensor_tensor(d1, ref, b1, ALU.subtract)
                    V.tensor_tensor(d2, b2, ref, ALU.subtract).then_inc(Z["s_D"], 1)

                def merge(k):
                    dve.wait_ge(Z["s_sc"], 8 * t + (k + 1))
                    if k == 0:
                        past(dve, Z["s_o"], t)
                        V.tensor_tensor(Sc[:], A[4][:, :].rearrange("p (h n) -> p h n", h=H),
                                        ident[:].unsqueeze(1).to_broadcast([P, H, P]), ALU.mult).then_inc(Z["s_mg"], 1)
                        return
                    h = LEVELS[k - 1]
                    dve.wait_ge(Z["s_mg"], 8 * t + k)
                    settle(dve)
                    _, dst, _ = halves(Sc[:], h)
                    V.copy_predicated(dst, mask[:, k - 1].rearrange("p (n b) -> p n b", b=h).unsqueeze(1).to_broadcast([P, H, 64 // h, h]),
                                      A[4 + k % 2][:, 0:H * 64].rearrange("p (h n b) -> p h n b", h=H, b=h)).then_inc(Z["s_mg"], 1)

                def level(k):
                    dve.wait_ge(Z["s_E"], 9 * t + (2 + k))
                    if k == 0:
                        past(dve, Z["s_kt"], t)
                        V.tensor_tensor(kd[:], Kt, Ee[:, 0], ALU.mult).then_inc(Z["s_kd"], 1)
                    else:
                        h = LEVELS[k - 1]
                        past(dve, Z["s_sc"], 8 * t + (k - 1))
                        k1, _, _ = halves(Kt, h)
                        _, q2, _ = halves(Qt, h)
                        e1, e2, _ = halves(Ee[:, k % 2], h)
                        kl1, _, _ = halves(KL[:, k % 2], h)
                        V.tensor_tensor(kl1, k1, e1, ALU.mult)
                        V.tensor_tensor(QL[:, k % 2].rearrange("p h (n b) -> p h n b", b=h), q2, e2, ALU.mult).then_inc(Z["s_QK"], 1)
                    if k + 2 < 8:
                        exponent(k + 2)
                    if k >= 1:
                        merge(k - 1)

                exponent(0)
                exponent(1)
                if last_tile is not None:
                    state(last_tile)
                level(0)
                level(1)
                if last_tile is not None:
                    normalise(last_tile)
                level(2)
                dve.wait_ge(Z["s_E"], 9 * t + 1)
                past(dve, Z["s_o"], t)
                V.tensor_tensor(qe[:], Qt, E0[:], ALU.mult).then_inc(Z["s_qe"], 1)
                V.tensor_copy(small[:, 112:116], E0[:, :, P - 1]).then_inc(Z["s_ebl"], 1)
                level(3)
                if last_tile is not None:
                    gate_o(last_tile)
                level(4)
                level(5)
                if last_tile is not None:
                    o_low(last_tile)
                level(6)
                level(7)
                merge(7)

            tile(0, None)
            with dve.Fori(1, NT) as t:
                own.enter(t, 1, 1)
                tile(t, t - 1)
            own.leave(NT)
            normalise(NT - 1)
            gate_o(NT - 1)
            o_low(NT - 1)

            for g in range(H):
                dve.wait_ge(Z["s_mh"], g + 1)
                V.tensor_tensor(ml[:, g], mixr[:, g], mh[:, g].bitcast(F32), ALU.subtract).then_inc(Z["s_ml"], 1)
            with dve.Fori(0, KC // 2) as pair:
                m = pair * 2
                own.enter(pair, 4)
                for b in range(2):
                    dve.wait_ge(Z["s_sg"], m + (b + 1))
                    for hf in range(2):
                        if hf:
                            dve.wait_ge(Z["s_mm"], m + (N_A + 1 + b))
                        else:
                            dve.wait_ge(Z["s_br"], m + (1 + b))
                        cs = slice(hf * HALF, (hf + 1) * HALF)
                        own.link(V.tensor_tensor(t12[:, 0], A[2 * hf][:, :], ghg[:, b, cs], ALU.mult))
                        V.tensor_tensor(t12[:, 1], A[2 * hf + 1][:, :], gpl[:, b, cs], ALU.mult).then_inc(Z["s_free"], 1)
                        dve.wait_ge(Z["s_free"], 2 * m + (N_A + 2 * b + hf + 1))
                        dve.wait_ge(Z["s_hn"], 2 * m + (16 + 2 * b + hf - 1))
                        V.tensor_tensor(valr[:, hf], t12[:, 0], t12[:, 1], ALU.add).then_inc(Z["s_bval"], 1)
                        dve.wait_ge(Z["s_bval"], 2 * m + (2 * b + hf + 1))
            own.leave(KC // 2)

            for n, r in enumerate((0, 2, 1, 3)):
                dve.wait_ge(Z["s_rowl"], 48 * (n + 1))
                if r == 2:
                    V.tensor_tensor(rows[:, r], rows[:, r], rtmp[:, 0], ALU.add).then_inc(Z["s_rows"], 1)
                else:
                    own.link(V.tensor_tensor(rows[:, r], rows[:, r], rtmp[:, 0], ALU.add))
                    V.scalar_tensor_tensor(rows[:, r], rows[:, r], 1.0 if r == 1 else 0.0, rtmp[:, 1], ALU.add, ALU.mult).then_inc(Z["s_rows"], 1)
            dve.wait_ge(Z["s_rows"], 4)

            def logits(t):
                dve.wait_ge(Z["s_rt"], t + 1)
                V.tensor_tensor(L[:, t], A[6][:, 0:G + E], brow[:], ALU.add).then_inc(Z["s_L"], 1)

            dve.wait_ge(Z["s_wr"], 64)
            for t in range(NT):
                b = t % 2
                dve.wait_ge(Z["s_mixsq"], t + 1)
                V.tensor_tensor(small[:, 82:83], small[:, 80:81], small[:, 81:82], ALU.add).then_inc(Z["s_mixsd"], 1)
                dve.wait_ge(Z["s_mt"], t + 1)
                rsqrt(small[:, 84:85], small[:, 83:84], small[:, 82:83], small[:, 85:86], 1.0 / D)
                for q in range(2):
                    cs = slice(q * HALF, (q + 1) * HALF)
                    last = V.scalar_tensor_tensor(mm_t[:, cs], A[2 * b + q][:, :], small[:, 84:85], rows[:, 0, cs], ALU.mult, ALU.mult)
                own.link(last)
                dve.wait_ge(Z[f"s_xr{b}"], 16 * (t // 2 + 1))
                if t >= 2:
                    dve.wait_ge(Z[f"s_hst{b}"], 16 * (t // 2))
                V.tensor_tensor(hh[:, b], mm_t[:], xr[:, b], ALU.add).then_inc(Z["s_h"], 1)
                dve.wait_ge(Z["s_hsd"], t + 1)
                rsqrt(small[:, 90:91], small[:, 89:90], small[:, 88:89], small[:, 91:92], 1.0 / D)
                own.link(V.scalar_tensor_tensor(mm_t[:], hh[:, b], small[:, 90:91], rows[:, 1], ALU.mult, ALU.mult))
                if t >= 2:
                    dve.wait_ge(Z[f"s_nst{b}"], 16 * (t // 2))
                    dve.wait_ge(Z["s_h2T"], 2 * (t - 1))
                V.tensor_tensor(hn2[:, b], mm_t[:], rows[:, 2], ALU.add).then_inc(Z["s_hn2"], 1)
                if t:
                    logits(t - 1)
            logits(NT - 1)

            dve.wait_ge(Z["s_L"], NT)
            for b in range(2):
                dve.wait_ge(Z[f"s_hst{b}"], 64)
                dve.wait_ge(Z[f"s_nst{b}"], 64)
            dve.wait_ge(Z["s_h2T"], 2 * NT)
            gl = L[:, :, 0:G]
            el_ = L[:, :, G:G + E].rearrange("p t (g e) -> p t g e", e=EG)

            def st(n, k=None):
                return rs_[:, n] if k is None else rs_[:, n, k]

            def bc(v, n):
                return v.unsqueeze(2).to_broadcast([P, NT, n])

            def first_max(prob, n, ramp, best, arg, onehot, tmp):
                own.link(V.tensor_reduce(best, prob, AX.X, ALU.max))
                own.link(V.tensor_tensor(tmp, prob, bc(best, n), ALU.is_ge))
                own.link(V.tensor_scalar(tmp, tmp, -99.0, 99.0, ALU.mult, ALU.add))
                own.link(V.tensor_tensor(tmp, tmp, ramp, ALU.add))
                own.link(V.tensor_reduce(arg, tmp, AX.X, ALU.min))
                own.link(V.tensor_tensor(onehot, ramp, bc(arg, n), ALU.is_equal))

            def softmax_rest(prob, n, total):
                own.link(V.tensor_reduce(total, prob, AX.X, ALU.add))
                own.link(V.reciprocal(total, total))
                own.link(V.tensor_tensor(prob, prob, bc(total, n), ALU.mult))

            gp = R[0][:, :, :, 0]
            own.link(V.tensor_reduce(st(0, 0), gl, AX.X, ALU.max))
            V.tensor_tensor(gp, gl, bc(st(0, 0), G), ALU.subtract).then_inc(Z["s_ge"], 1)
            dve.wait_ge(Z["s_ge"], 2)
            softmax_rest(gp, G, st(0, 0))
            dve.wait_ge(Z["s_iota"], 2)
            rampG = iotaC[:, 0:G].unsqueeze(1).to_broadcast([P, NT, G])
            rampE = iotaC[:, 0:EG].unsqueeze(1).to_broadcast([P, NT, EG])
            ohg = R[1][:, :, :, 0]
            first_max(gp, G, rampG, st(1, 0), st(2, 0), ohg, R[3][:, :, :, 0])
            sel = R[2][:, :, 0]
            own.link(V.tensor_tensor(R[3][:], el_, ohg.unsqueeze(3).to_broadcast([P, NT, G, EG]), ALU.mult))
            own.link(V.tensor_reduce(sel, R[3][:].rearrange("p t g e -> p t e g"), AX.X, ALU.add))
            own.link(V.tensor_reduce(st(3, 0), sel, AX.X, ALU.max))
            V.tensor_tensor(sel, sel, bc(st(3, 0), EG), ALU.subtract).then_inc(Z["s_ge"], 1)
            dve.wait_ge(Z["s_ge"], 4)
            softmax_rest(sel, EG, st(3, 0))
            oh1, oh2, tmp8 = R[4][:, :, 0], R[5][:, :, 0], R[3][:, :, 0]
            first_max(sel, EG, rampE, st(4, 0), st(5, 0), oh1, tmp8)
            own.link(V.scalar_tensor_tensor(sel, oh1, -2.0, sel, ALU.mult, ALU.add))
            first_max(sel, EG, rampE, st(4, 1), st(5, 1), oh2, tmp8)
            own.link(V.tensor_tensor(st(6, 0), st(4, 0), st(4, 1), ALU.add))
            own.link(V.reciprocal(st(6, 0), st(6, 0)))
            for k in range(2):
                own.link(V.tensor_tensor(st(7, k), st(1, 0), st(4, k), ALU.mult))
                own.link(V.tensor_tensor(wts[:, k], st(7, k), st(6, 0), ALU.mult))
                own.link(V.scalar_tensor_tensor(st(8, k), st(2, 0), float(EG), st(5, k), ALU.mult, ALU.add))
            M1, M2, M = R[8], R[9], R[7]
            for Mk, o_ in ((M1, oh1), (M2, oh2)):
                own.link(V.tensor_tensor(Mk[:], ohg.unsqueeze(3).to_broadcast([P, NT, G, EG]),
                                         o_.unsqueeze(2).to_broadcast([P, NT, G, EG]), ALU.mult))
            own.link(V.tensor_tensor(M[:], M1[:], M2[:], ALU.add))
            V.tensor_reduce(c32[:, 0, :], M[:].rearrange("p t g e -> p (g e) t"), AX.X, ALU.add).then_inc(Z["s_M"], 1)
            dve.wait_ge(Z["s_pos"], 1)
            pos = A[0][:, 0:NT * E].rearrange("p (t e) -> p t e", e=E)
            T = R[10][:].rearrange("p t g e -> p t (g e)")
            for k, Mk in enumerate((M1, M2)):
                own.link(V.tensor_tensor(T, pos, Mk[:].rearrange("p t g e -> p t (g e)"), ALU.mult))
                own.link(V.tensor_reduce(st(9, k), T, AX.X, ALU.add))
            own.link(V.memset(st(10), 0.0))
            for j in range(1, NJ + 1):
                own.link(V.scalar_tensor_tensor(st(10), st(9), float(j * BLK), st(10), ALU.is_ge, ALU.add))
            own.link(V.scalar_tensor_tensor(st(11), st(10), float(-BLK), st(9), ALU.mult, ALU.add))
            own.link(V.tensor_copy(c32[:, 1], A[1][:, 0:E]))
            own.link(V.memset(c32[:, 2], 0.0))
            own.link(V.memset(c32[:, 3], 1.0))
            for j in range(1, NJ + 1):
                own.link(V.scalar_tensor_tensor(c32[:, 2], c32[:, 1], float(j * BLK + 1), c32[:, 2], ALU.is_ge, ALU.add))
            own.link(V.tensor_tensor_scan(c32[:, 5], c32[:, 3], c32[:, 2], 0.0, ALU.mult, ALU.add))
            own.link(V.tensor_tensor(c32[:, 4], c32[:, 5], c32[:, 2], ALU.subtract))
            for k, Mk in enumerate((M1, M2)):
                own.link(V.tensor_tensor(T, Mk[:].rearrange("p t g e -> p t (g e)"), c32[:, 4:5, :].to_broadcast([P, NT, E]), ALU.mult))
                own.link(V.tensor_reduce(st(12, k), T, AX.X, ALU.add))
            own.link(V.tensor_tensor(st(13), st(12), st(10), ALU.add))
            own.link(V.tensor_scalar(st(13), st(13), float(E - 1), None, ALU.add))
            own.link(V.tensor_tensor(st(13), st(13), st(8), ALU.subtract))
            own.link(V.tensor_scalar(st(14), st(10), 1.0, None, ALU.is_ge))
            own.link(V.tensor_tensor(st(13), st(13), st(14), ALU.mult))
            own.link(V.tensor_tensor(st(13), st(13), st(8), ALU.add))
            own.link(V.scalar_tensor_tensor(st(15), st(13), float(BLK), st(11), ALU.mult, ALU.add))
            own.link(V.tensor_copy(dest[:], st(15)))
            own.link(V.tensor_copy(ovt[0:1, 0:1], c32[0:1, 5, E - 1:E]))
            own.link(V.tensor_tensor(ovcmp[0:1], c32[0:1, 5:6, :].to_broadcast([1, NOV, E]),
                                     iotaC[0:1, 0:NOV].unsqueeze(2).to_broadcast([1, NOV, E]), ALU.is_le))
            own.link(V.tensor_reduce(ovf[0:1, 0:NOV], ovcmp[0:1], AX.X, ALU.add))
            own.link(V.tensor_scalar(ovf[0:1, 0:NOV], ovf[0:1, 0:NOV], float(E - 1), None, ALU.min))
            V.tensor_copy(ovt[0:1, 1:1 + NOV], ovf[0:1, 0:NOV]).then_inc(Z["s_tabd"], 1)
            for n in range(2 * NT):
                t, k = divmod(n, 2)
                if n >= 2:
                    dve.wait_ge(Z["s_slots"], n - 1)
                V.tensor_scalar(Aoh[:, n % 2], iotaS[:], rs_[:, 11, k, t:t + 1], None, ALU.is_equal)
                V.tensor_scalar(Boh[:, n % 2], iotaC[:], rs_[:, 13, k, t:t + 1], small[:, 148 + t:149 + t], ALU.is_equal, ALU.mult).then_inc(Z["s_AB"], 1)
            dve.wait_ge(Z["s_slots"], 2 * NT)
            V.tensor_copy(idxt[0:BLK, 0:NCOL], A[2][0:BLK, 0:NCOL]).then_inc(Z["s_tabd"], 1)

            def lo(n, slot):
                dve.wait_ge(Z["s_phi"], n + 1)
                V.tensor_tensor(el[:, slot], raw6[:, slot], eh[:, slot].bitcast(F32), ALU.subtract).then_inc(Z["s_plo"], 1)

            def x_low(cnt, b, q):
                dve.wait_ge(Z["s_xTh"], 2 * cnt + (q + 1))
                V.tensor_tensor(xTl[:, b, 4 * q:4 * q + 4].rearrange("p k n -> p (k n)"), A[4][:, :],
                                xTh[:, b, 4 * q:4 * q + 4].rearrange("p k n -> p (k n)").bitcast(F32), ALU.subtract).then_inc(Z["s_xTl"], 1)

            def a_prod(e, b):
                dve.wait_ge(Z["s_sil"], e + 1)
                V.tensor_tensor(aa[:, b], A[2 * b + 1][:, :], sil[:], ALU.mult).then_inc(Z["s_a"], 1)

            def a_low(e, b):
                dve.wait_ge(Z["s_aTh"], e + 1)
                V.tensor_tensor(aTl[:, b].rearrange("p k n -> p (k n)"), A[5][:, :],
                                aTh[:, b].rearrange("p k n -> p (k n)").bitcast(F32), ALU.subtract).then_inc(Z["s_aTl"], 1)

            for n in range(6):
                lo(n, n)
            for e in range(2):
                for q in range(2):
                    x_low(e, e, q)

            def step(e, i, b, last_x=False):
                n0 = 4 + 6 * (1 - b)

                def l_(j):
                    k = n0 + j
                    lo(i * 12 + k, k % 6)
                a_prod(e - 1, 1 - b)
                l_(2)
                l_(3)
                if not last_x:
                    x_low(e + 1, 1 - b, 0)
                l_(4)
                l_(5)
                a_low(e - 1, 1 - b)
                if not last_x:
                    x_low(e + 1, 1 - b, 1)
                l_(6)
                l_(7)

            with dve.Fori(0, E // 2 - 1) as i:
                step(i * 2 + 1, i, 1)
                step(i * 2 + 2, i, 0)
            step(E - 1, E // 2 - 1, 1, last_x=True)
            a_prod(E - 1, 1)
            a_low(E - 1, 1)
            nov = dve.value_load(ovt[0:1, 0:1], min_val=0, max_val=NOV)
            with dve.If(nov > 0):
                with dve.Fori(0, NOV) as j:
                    with dve.If(nov > j):
                        for q in range(2):
                            x_low(j + E, 0, q)
                        for k in range(6):
                            lo(j * 6 + (6 * E + k), k)
                        a_prod(j + E, 0)
                        a_low(j + E, 0)

            for t in range(NT):
                b = t % 2
                dve.wait_ge(Z[f"s_Y{b}"], 32 * (t // 2 + 1))
                if t >= 2:
                    dve.wait_ge(Z[f"s_out{b}"], 16 * (t // 2))
                if t == 0:
                    dve.wait_ge(Z["s_ovd"], 1)
                own.link(V.tensor_scalar(yo[:, b], Y1[:, b], wts[:, 0, t:t + 1], None, ALU.mult))
                V.scalar_tensor_tensor(yo[:, b], Y2[:, b], wts[:, 1, t:t + 1], yo[:, b], ALU.mult, ALU.add).then_inc(Z["s_ysum"], 1)
                dve.wait_ge(Z["s_ysd"], t + 1)
                rsqrt(small[:, 100:101], small[:, 98 + b:99 + b], small[:, 96 + b:97 + b], small[:, 101:102], 1.0 / D)
                own.link(V.scalar_tensor_tensor(yo[:, b], yo[:, b], small[:, 100:101], rows[:, 3], ALU.mult, ALU.mult))
                dve.wait_ge(Z[f"s_hb{b}"], 16 * (t // 2 + 1))
                V.tensor_tensor(yo[:, b], yo[:, b], hb[:, b], ALU.add).then_inc(Z["s_fin"], 1)

        @block.gpsimd
        def _(pool):
            own = Chain(pool, Z["s_pool_own"])
            PL = nc.gpsimd
            PL.memset(ident[:], 0.0).then_inc(Z["s_ident"], 1)
            pool.wait_ge(Z["s_ident"], 1)
            PL.affine_select(out=ident[:], in_=ident[:], compare_op=ALU.not_equal, fill=1.0, base=0,
                             pattern=[[-1, P]], channel_multiplier=1).then_inc(Z["s_ident"], 1)
            own.link(PL.iota(small[:, 128:144], pattern=[[1, 16]], base=0, channel_multiplier=0, allow_small_or_imprecise_dtypes=True))
            own.link(PL.iota(small[:, 148:156], pattern=[[P, NT]], base=0, channel_multiplier=1, allow_small_or_imprecise_dtypes=True))
            own.link(PL.iota(iS[:], pattern=[[0, P]], base=0, channel_multiplier=1))
            PL.iota(iT[:], pattern=[[1, P]], base=0, channel_multiplier=0).then_inc(Z["s_iota"], 1)

            for n in range(16):
                hf, k = divmod(n, KC)
                pool.wait_ge(Z["s_hh"], n + 1)
                PL.tensor_tensor(hnl[:, k, bass.ts(hf, HALF)], valr[:, n % 2], hnh[:, k, bass.ts(hf, HALF)].bitcast(F32),
                                 ALU.subtract).then_inc(Z["s_hn"], 1)

            def low(cn, b):
                pool.wait_ge(Z["s_hi"], cn + 1)
                PL.tensor_tensor(wl[:, b], raw[:, b], wh[:, b].bitcast(F32), ALU.subtract).then_inc(Z["s_lo"], 1)

            with pool.Fori(0, N_A // 2) as pair:
                cn = pair * 2
                for b in range(2):
                    low(cn + b, b)
            low(N_A, 0)
            low(N_A + 1, 1)

            def branch(m, more):
                for b in range(2):
                    for hf in range(2):
                        pool.wait_ge(Z["s_mTh"], 2 * m + (2 * b + hf + 1))
                        dst = (slice(None), bass.ds(m + b, 1), bass.ts(hf, HALF))
                        PL.tensor_tensor(hnl[dst].rearrange("p a n -> p (a n)"), valr[:, hf],
                                         hnh[dst].rearrange("p a n -> p (a n)").bitcast(F32), ALU.subtract).then_inc(Z["s_hn"], 1)
                    if more:
                        low(m + (N_A + 2 + b), b)

            with pool.Fori(0, KC // 2 - 1) as pair:
                branch(pair * 2, True)
            branch(KC - 2, False)
            for k in range(KC):
                pool.wait_ge(Z["s_hi"], N_CH + k + 1)
                PL.tensor_tensor(wol[:, k], raw[:, k % 2].rearrange("p k n -> p (k n)"), woh[:, k].bitcast(F32), ALU.subtract).then_inc(Z["s_lo"], 1)
            pool.wait_ge(Z["s_hn2"], NT)
            for b in range(2):
                pool.wait_ge(Z[f"s_hst{b}"], 64)
                pool.wait_ge(Z[f"s_nst{b}"], 64)
            pool.wait_ge(Z["s_h2T"], 2 * NT)
            own.link(PL.iota(iotaS[:], pattern=[[1, P]], base=0, channel_multiplier=0, allow_small_or_imprecise_dtypes=True))
            own.link(PL.iota(iotaC[:], pattern=[[1, 64]], base=0, channel_multiplier=0, allow_small_or_imprecise_dtypes=True))
            own.link(PL.memset(tri[:], 1.0))
            PL.affine_select(out=tri[:], in_=tri[:], compare_op=ALU.is_gt, fill=0.0, base=0, pattern=[[1, P]],
                             channel_multiplier=-1).then_inc(Z["s_iota"], 1)

            pool.wait_ge(Z["s_tabd"], 2)

            def gather(cnt, col, b):
                PL.tensor_copy(idxc[0:BLK, b], idxt[0:BLK, col]).then_inc(Z["s_idx"], 1)
                pool.wait_ge(Z["s_idx"], cnt + 1)
                settle(pool)
                PL.indirect_dma_start(out=xg[0:BLK, b], out_offset=None, in_=hn2_d[:, :],
                                      in_offset=bass.IndirectOffsetOnAxis(ap=idxc[0:BLK, b], axis=0)).then_inc(Z[f"s_xg{b}"], 16)

            gather(0, slice(0, 1), 0)
            gather(1, slice(1, 2), 1)
            with pool.Fori(0, E // 2 - 1) as i:
                for b in range(2):
                    e = i * 2 + (2 + b)
                    pool.wait_ge(Z["s_xTp"], 4 * i + (2 * b + 2))
                    gather(e, bass.ds(e, 1), b)
            nov = pool.value_load(ovt[0:1, 0:1], min_val=0, max_val=NOV)
            with pool.If(nov > 0):
                with pool.Fori(0, NOV) as j:
                    with pool.If(nov > j):
                        pool.wait_ge(Z["s_xTp"], j * 2 + 2 * E)
                        gather(j + E, bass.ds(j + E, 1), 0)
            pool.wait_ge(Z["s_ovd"], 1)

            def rows_of(source):
                for t in range(NT):
                    b = t % 2
                    if t >= 2:
                        pool.wait_ge(Z["s_ysum"], t - 1)
                    for k, Y in enumerate((Y1, Y2)):
                        PL.indirect_dma_start(out=Y[:, b], out_offset=None, in_=source,
                                              in_offset=bass.IndirectOffsetOnAxis(ap=dest[:, k, t:t + 1], axis=0)).then_inc(Z[f"s_Y{b}"], 16)

            with pool.If(nov > 0):
                rows_of(y_d[:, :])
            with pool.If(nov < 1):
                rows_of(y_d[0:E * BLK, :])


_INS = ['x', 'c', 'w_ada', 'b_ada', 'g_pre_mix', 'g_post_mix', 'w_in', 'hg_lb_logits', 'hg_norm_g', 'pool_w', 'pool_scale',
        'w_branch_hg', 'w_branch_pool', 'w_gate', 'b_gate', 'w_out', 'g_pre_ffn', 'g_post_ffn', 'w_router_group',
        'b_router_group', 'w_router_expert', 'b_router_expert', 'w_exp_gate', 'w_exp_up', 'w_exp_down']
_OUTS = [((1, 1024, 1024), 'float32')]


def kernel(**inputs):
    import numpy as _np
    import concourse.bacc as _bacc
    from concourse import mybir as _mybir
    from concourse.bass_utils import run_bass_kernel_spmd as _run

    nc = _bacc.Bacc("TRN2", target_bir_lowering=False, num_devices=1)
    arrays, args = {}, []
    for name in _INS:
        a = _np.ascontiguousarray(inputs[name])
        arrays[f"in_{name}_dram"] = a
        args.append(nc.dram_tensor(f"in_{name}_dram", a.shape, _mybir.dt.from_np(a.dtype), kind="ExternalInput").ap())
    for i, (shape, dtype) in enumerate(_OUTS):
        dt = _mybir.dt.from_np(_np.dtype(dtype))
        args.append(nc.dram_tensor(f"out_{i}_dram", shape, dt, kind="ExternalOutput").ap())
    build(nc, *args)
    r = _run(nc, [arrays], core_ids=[0])
    got = tuple(r.results[0][f"out_{i}_dram"] for i in range(len(_OUTS)))
    return got[0]
```

```python
from contextlib import ExitStack

import concourse.bass as bass
from concourse import mybir

F32 = mybir.dt.float32
F32R = mybir.dt.float32r
I32 = mybir.dt.int32
ALU = mybir.AluOpType
ACT = mybir.ActivationFunctionType
AX = mybir.AxisListType

P = 128
D = 1024
S = 1024
KC = D // P
NT = S // P
HALF = 512
H = 4
EPS = 1e-6
G, EG = 4, 8
E = G * EG
FF = 512
BLK = 128
NJ = (S - 1) // BLK
NOV = (2 * S - 1) // BLK
NCOL = E + NOV
LEVELS = [1, 2, 4, 8, 16, 32, 64]
KB = 1024

W_IN_ORDER = [4, 8, 16, 0, 12]
N_IN = 20
N_A = N_IN + 16
N_CH = N_A + KC

C_COND, C_BADA, C_GPRE, C_BGATE, C_LB0, C_LB1, C_NG, C_PS, N_VEC = 0, 8, 24, 32, 48, 52, 56, 60, 64


class Chain:

    def __init__(self, eng, sem):
        self.eng, self.sem, self.n, self.steps = eng, sem, 0, 0

    def link(self, ins):
        self.n = self.n + 1
        self.steps += 1
        ins.then_inc(self.sem, 1)
        self.eng.wait_ge(self.sem, self.n)

    def enter(self, i, per, first=0):
        self.base, self.per, self.steps = self.n - first * per, per, 0
        self.n = i * per + self.base

    def leave(self, end):
        assert self.steps == self.per, (self.steps, self.per)
        self.n = self.base + end * self.per


def past(eng, sem, count):
    if not (isinstance(count, int) and count <= 0):
        eng.wait_ge(sem, count)


def build(nc, x, c, w_ada, b_ada, g_pre_mix, g_post_mix, w_in, lb_logits, hg_norm_g, pool_w, pool_scale,
          w_bhg, w_bpool, w_gate, b_gate, w_out, g_pre_ffn, g_post_ffn, w_rg, b_rg, w_re, b_re,
          w_eg, w_eu, w_ed, out):
    with ExitStack() as ctx:
        def at(name, shape, dt, kb):
            return nc.alloc_sbuf_tensor_at(name, shape, dt, offset=int(kb * KB))

        def sem(name):
            return ctx.enter_context(nc.semaphore(name))

        def dram(name, shape):
            return nc.dram_tensor(name, shape, F32, kind="Internal").ap()

        o = -(-nc.sbuf_base // KB)
        ident = at("ident", [P, P], F32, o + 0)
        ones = at("ones", [P, P], F32, o + 0.5)
        mask = at("mask", [P, 7, 64], I32, o + 1)
        cols = at("cols", [P, N_VEC], F32, o + 2.75)
        small = at("small", [P, 192], F32, o + 3)
        valr = at("valr", [P, 2, HALF], F32, o + 4)
        win2 = at("win2", [P, S], F32, o + 4)
        rowr = at("rowr", [1, HALF], F32, o + 8)
        hnh = at("hnh", [P, KC, S], F32R, o + 10)
        hnl = at("hnl", [P, KC, S], F32R, o + 42)
        raw = at("raw", [P, 2, KC, P], F32, o + 74)
        wh = at("wh", [P, 2, KC, P], F32R, o + 82)
        wl = at("wl", [P, 2, KC, P], F32R, o + 90)
        xt = at("xt", [P, NT, D], F32, o + 98)
        adab = at("adab", [P, 4, 4, HALF], F32, o + 130)
        acc0 = at("acc0", [P, 4, HALF], F32, o + 162)
        acc1 = at("acc1", [P, 2, HALF], F32, o + 170)
        vecs = at("vecs", [N_VEC, P], F32, o + 8)
        xorm = at("xorm", [P, P], I32, o + 174)
        iS = at("iS", [P, P], I32, o + 174.5)
        iT = at("iT", [P, P], I32, o + 175)
        mtmp = at("mtmp", [P, 64], F32, o + 175.5)
        Bc = at("Bc", [P, H, S], F32, o + 98)
        Kk = at("Kk", [P, H, S], F32, o + 114)
        Qq = at("Qq", [P, H, S], F32, o + 130)
        Vv = at("Vv", [P, NT, HALF], F32, o + 146)
        scanm = at("scanm", [P, S], F32, o + 162)
        win1 = at("win1", [P, S], F32, o + 166)
        vT = at("vT", [P, H, S], F32, o + 174)
        ub = at("ub", [P, H, S], F32, o + 190)
        pt = at("pt", [P, 2, S], F32, o + 174)
        gt = at("gt", [P, 2, S], F32, o + 194)
        poolw = at("poolw", [P, H, P], F32, o + 8)
        Dd = at("Dd", [P, 2, H, P], F32, o + 162)
        Ee = at("Ee", [P, 2, H, P], F32, o + 166)
        E0 = at("E0", [P, H, P], F32, o + 170)
        QL = at("QL", [P, 2, H, 64], F32, o + 172)
        KL = at("KL", [P, 2, H, P], F32, o + 174)
        Kc = at("Kc", [P, H, P], F32, o + 178)
        Sc = at("Sc", [P, H, P], F32, o + 180)
        qe = at("qe", [P, H, P], F32, o + 182)
        kd = at("kd", [P, H, P], F32, o + 184)
        kdN = at("kdN", [P, H, P], F32, o + 186)
        St = at("St", [P, H, P], F32, o + 188)
        on = at("on", [P, H, P], F32, o + 190)
        ov = at("ov", [P, H, P], F32, o + 192)
        gs = at("gs", [P, H, P], F32, o + 202)
        sqs = at("sqs", [P, H, P], F32, o + 204)
        oh = at("oh", [P, H, S], F32R, o + 98)
        ol = at("ol", [P, H, S], F32R, o + 114)
        mixr = at("mixr", [P, H, S], F32, o + 130)
        mh = at("mh", [P, H, S], F32R, o + 146)
        ml = at("ml", [P, H, S], F32R, o + 162)
        ghg = at("ghg", [P, 2, S], F32, o + 178)
        gpl = at("gpl", [P, 2, S], F32, o + 186)
        t12 = at("t12", [P, 2, HALF], F32, o + 202)
        woh = at("woh", [P, KC, D], F32R, o + 98)
        wol = at("wol", [P, KC, D], F32R, o + 130)
        rows = at("rows", [P, 4, D], F32, o + 162)
        wraw03 = at("wraw03", [P, 4, D], F32, o + 130)
        wraw45 = at("wraw45", [P, 2, D], F32, o + 194)
        xr = at("xr", [P, 2, D], F32, o + 178)
        hh = at("hh", [P, 2, D], F32, o + 186)
        hn2 = at("hn2", [P, 2, D], F32, o + 194)
        h2T = at("h2T", [P, KC, P], F32, o + 82)
        wr = at("wr", [P, KC, G + E], F32, o + 90)
        brow = at("brow", [P, G + E], F32, o + 91.5)
        junk = at("junk", [P, D], F32, o + 92)
        mm_t = at("mm_t", [P, D], F32, o + 202)
        L = at("L", [P, NT, G + E], F32, o + 96)
        R = [at(f"R{k}", [P, NT, G, EG], F32, o + 178 + k) for k in range(12)]
        rs_ = at("rs_", [P, 24, 2, NT], F32, o + 190)
        c32 = at("c32", [P, 8, E], F32, o + 192)
        iotaS = at("iotaS", [P, P], F32, o + 193)
        iotaC = at("iotaC", [P, 64], F32, o + 193.5)
        Aoh = at("Aoh", [P, 2, P], F32, o + 194)
        Boh = at("Boh", [P, 2, 64], F32, o + 195)
        tri = at("tri", [P, P], F32, o + 195.5)
        ovcmp = at("ovcmp", [P, NOV, E], F32, o + 196)
        wts = at("wts", [P, 2, NT], F32, o + 170)
        dest = at("dest", [P, 2, NT], I32, o + 170.25)
        idxt = at("idxt", [P, 64], I32, o + 170.5)
        idxc = at("idxc", [P, 2, 1], I32, o + 171)
        ovt = at("ovt", [1, 64], I32, o + 171.25)
        ovf = at("ovf", [1, 64], F32, o + 171.5)
        raw6 = at("raw6", [P, 6, 4, HALF], F32, o + 10)
        eh = at("eh", [P, 6, 4, HALF], F32R, o + 58)
        el = at("el", [P, 6, 4, HALF], F32R, o + 106)
        xTh = at("xTh", [P, 2, KC, P], F32R, o + 154)
        xTl = at("xTl", [P, 2, KC, P], F32R, o + 162)
        sil = at("sil", [P, HALF], F32, o + 172)
        xg = at("xg", [P, 2, D], F32, o + 178)
        aa = at("aa", [P, 2, HALF], F32, o + 186)
        aTh = at("aTh", [P, 2, 4, P], F32R, o + 190)
        aTl = at("aTl", [P, 2, 4, P], F32R, o + 194)
        yy = at("yy", [P, D], F32, o + 198)
        Y1 = at("Y1", [P, 4, D], F32, o + 10)
        Y2 = at("Y2", [P, 4, D], F32, o + 26)
        hb = at("hb", [P, 4, D], F32, o + 42)
        yo = at("yo", [P, 4, D], F32, o + 58)
        ysq = at("ysq", [P, D], F32, o + 74)

        A = [ctx.enter_context(nc.psum_tensor(f"bank{k}", [P, HALF], F32)) for k in range(8)]

        spill = dram("spill", (20 + 4, P, S))
        ada_d = dram("ada_d", (8, HALF))
        h_d = dram("h_d", (S, D))
        hn2_d = dram("hn2_d", (S, D))
        y_d = dram("y_d", (NCOL * BLK, D))

        xv = x.rearrange("b (t p) d -> t p (b d)", p=P)
        outv = out.rearrange("b (t p) d -> t p (b d)", p=P)
        adav = w_ada[0].rearrange("(k p) n -> p k n", p=P)
        winv = w_in[0].rearrange("(k p) n -> p k n", p=P)
        wgav = w_gate[0].rearrange("(k p) n -> p k n", p=P)
        wbh = w_bhg[0].rearrange("(k p) n -> p k n", p=P)
        wbp = w_bpool[0].rearrange("(k p) n -> p k n", p=P)
        wov = w_out[0].rearrange("(k p) n -> k p n", p=P)
        egv = w_eg[0].rearrange("e (k p) n -> e p k n", p=P)
        euv = w_eu[0].rearrange("e (k p) n -> e p k n", p=P)
        edv = w_ed[0].rearrange("e (k p) n -> e p k n", p=P)

        names = """s_vec s_vecT s_cols s_cond s_x s_ssq s_sd s_xs s_xT s_val s_hh s_hn s_ident s_ones s_acc s_mod
            s_modc s_adam s_rowc s_rowst s_raw0 s_raw1 s_hi s_lo s_mm s_free s_ln s_B s_vt s_ve s_pool s_pm
            s_pe s_lbx s_pw s_const s_mask s_kc s_E s_D s_qe s_kd s_QK s_sc s_mg s_kt s_kn s_st s_S s_o s_osq
            s_osd s_on s_ot s_oval s_oh s_ol s_gs s_mixr s_mh s_ml s_gl0 s_gl1 s_br s_bval s_mTh s_rowl s_xr0
            s_xr1 s_wo s_mixsq s_mixsd s_h s_hst0 s_hst1 s_hsq s_hn2 s_nst0 s_nst1 s_h2T s_h2e s_rt s_L s_wr
            s_ge s_M s_pos s_AB s_slots s_tabd s_iota s_idx s_xg0 s_xg1 s_xTp s_xTh s_xTl s_phi s_plo s_pc
            s_sil s_a s_aT s_aTh s_aTl s_ycp s_yst s_y1 s_yn s_ysum s_ysq s_ysd s_fin s_gst0 s_gst1 s_ebl
            s_ovd s_dve s_act s_pool_own s_settled s_sg s_bg s_woh s_wolv s_wolp s_msd""".split()
        Z = {n: sem(n) for n in names}
        s_ada = [sem(f"s_ada{k}") for k in range(4)]
        s_wraw = [sem(f"s_wraw{k}") for k in range(KC)]
        s_Y = [sem(f"s_Y{k}") for k in range(4)]
        s_hb = [sem(f"s_hb{k}") for k in range(4)]
        s_out = [sem(f"s_out{k}") for k in range(4)]
        s_r6 = [sem(f"s_r6_{k}") for k in range(6)]

        def wraw(k):
            if k < 4:
                return wraw03[:, k]
            return wraw45[:, k - 4] if k < 6 else raw[:, k - 6].rearrange("p k n -> p (k n)")

        POOL_ROWS = [2, 5, 7]
        DVE_ROWS = [k for k in range(KC) if k not in POOL_ROWS]
        gains = [g_post_mix, None, g_pre_ffn, g_post_ffn]

        block = ctx.enter_context(nc.Block())

        def settle(eng):
            eng.sem_inc(Z["s_settled"], 1)

        def one(view):
            return view.rearrange("a p n -> p (a n)")

        @block.sync
        def _(sp):
            def vec(lo, n, src):
                sp.dma_start(vecs[lo:lo + n, :], src).then_inc(Z["s_vec"], 16)

            vec(C_COND, 8, c.rearrange("a (j p) -> (a j) p", p=P))
            vec(C_BADA, 16, b_ada[0:1, 0:2 * D].rearrange("a (j p) -> (a j) p", p=P))
            vec(C_GPRE, 8, g_pre_mix.rearrange("a (j p) -> (a j) p", p=P))
            vec(C_BGATE, 16, b_gate.rearrange("a (j p) -> (a j) p", p=P))
            vec(C_LB0, 8, lb_logits.rearrange("a (j p) -> (a j) p", p=P))
            vec(C_NG, 4, hg_norm_g.rearrange("a (j p) -> (a j) p", p=P))
            vec(C_PS, 4, pool_scale.rearrange("a (j p) -> (a j) p", p=P))

            def ada(piece, slot, first=False):
                for k in range(2):
                    if not first:
                        sp.wait_ge(Z["s_acc"], piece - 1)
                    sp.dma_start(adab[:, slot + k], adav[:, 4 * k:4 * k + 4, bass.ts(piece, HALF)]).then_inc(
                        s_ada[slot + k], 16)

            ada(0, 0, True)
            ada(1, 2, True)
            ada(2, 0)
            ada(3, 2)

            def chunk(cn, slot, top, bottom, wait=True):
                if wait:
                    sp.wait_ge(Z["s_lo"], cn - 1)
                sp.dma_start(raw[:, slot, 0:4], top).then_inc(Z[f"s_raw{slot}"], 16)
                sp.dma_start(raw[:, slot, 4:8], bottom).then_inc(Z[f"s_raw{slot}"], 16)

            def chunk_of(view, cn, slot, col, wait=True):
                chunk(cn, slot, view[:, 0:4, bass.ts(col, P)], view[:, 4:8, bass.ts(col, P)], wait)

            chunk_of(winv, 0, 0, W_IN_ORDER[0], False)
            chunk_of(winv, 1, 1, W_IN_ORDER[0] + 1, False)
            for cn in range(2, 10):
                chunk_of(winv, cn, cn % 2, W_IN_ORDER[cn // 4] + cn % 4)
                ada(cn + 2, 2 * (cn % 2))
            chunk_of(winv, 10, 0, W_IN_ORDER[2] + 2)
            chunk_of(winv, 11, 1, W_IN_ORDER[2] + 3)
            for kind in (3, 4):
                with sp.Fori(0, 4 // 2) as pair:
                    j = pair * 2
                    for b in range(2):
                        chunk_of(winv, j + (4 * kind + b), b, j + (W_IN_ORDER[kind] + b))
                if kind == 3:
                    sp.wait_ge(Z["s_rowst"], 16 * 8)
                    sp.dma_start(poolw[:], pool_w[0].rearrange("g p n -> p g n")).then_inc(Z["s_pw"], 16)
            def gates(t):
                for b in range(2):
                    chunk_of(wgav, t * 2 + (N_IN + b), b, t * 2 + b)
                sp.wait_ge(Z["s_gst0"], 16 * 4)
                sp.wait_ge(Z["s_gst1"], 16 * 4)
                past(sp, Z["s_oval"], t)
                sp.dma_start(gs[:], spill[4:8, :, bass.ts(t, P)].rearrange("h p n -> p h n")).then_inc(Z["s_gs"], 16)

            gates(0)
            with sp.Fori(1, NT) as t:
                gates(t)
            chunk(N_A, 0, wbh[:, :, 0:P], wbp[:, :, 0:P])
            chunk(N_A + 1, 1, wbh[:, :, P:2 * P], wbp[:, :, P:2 * P])
            for n, (first, end) in enumerate(((0, S - P), (S - P, S))):
                sp.wait_ge(Z["s_o"], NT - 1 + n)
                sp.dma_start(mixr[:, :, first:end], spill[0:4, :, first:end].rearrange("h p n -> p h n")).then_inc(Z["s_mixr"], 16)
            sp.wait_ge(Z["s_ol"], NT)
            sp.wait_ge(Z["s_gst0"], 16 * 12)
            sp.wait_ge(Z["s_gst1"], 16 * 12)

            def branch(m, more):
                for b in range(2):
                    sp.wait_ge(Z["s_free"], 2 * m + (N_A + 2 * b - 2))
                    sp.dma_start(ghg[:, b], one(spill[bass.ds(m + (8 + b), 1)])).then_inc(Z[f"s_gl{b}"], 16)
                    sp.dma_start(gpl[:, b], one(spill[bass.ds(m + (16 + b), 1)])).then_inc(Z[f"s_gl{b}"], 16)
                    if more:
                        at_ = bass.ts(m + (b + 2), P)
                        chunk(m + (N_A + b + 2), b, wbh[:, :, at_], wbp[:, :, at_])

            with sp.Fori(0, KC // 2 - 1) as pair:
                branch(pair * 2, True)
            sp.wait_ge(Z["s_mh"], H)
            sp.wait_ge(Z["s_ml"], H)

            def w_out_row(k):
                sp.dma_start(wraw(k), wov[k]).then_inc(s_wraw[k], 16)

            for k in range(6):
                w_out_row(k)
            branch(KC - 2, False)
            sp.wait_ge(Z["s_lo"], N_CH)
            w_out_row(6)
            w_out_row(7)
            sp.wait_ge(Z["s_mm"], N_CH)
            for r, piece in ((0, 0), (1, 4), (2, 2), (3, 6)):
                sp.dma_start(rows[:, r], ada_d[piece:piece + 2, :].rearrange("a n -> (a n)").partition_broadcast(P)).then_inc(Z["s_rowl"], 16)
            sp.wait_ge(Z["s_free"], N_A + 2 * KC)
            for t in range(2):
                sp.dma_start(xr[:, t], xv[t]).then_inc(Z[f"s_xr{t}"], 16)
            sp.dma_start(wr[:, :, 0:G], w_rg[0].rearrange("(k p) n -> p k n", p=P)).then_inc(Z["s_wr"], 16)
            sp.dma_start(wr[:, :, G:G + E], w_re[0].rearrange("(k p) n -> p k n", p=P)).then_inc(Z["s_wr"], 16)
            sp.dma_start(brow[:, 0:G], b_rg[0].partition_broadcast(P)).then_inc(Z["s_wr"], 16)
            sp.dma_start(brow[:, G:G + E], b_re[0].partition_broadcast(P)).then_inc(Z["s_wr"], 16)
            for t in range(NT + 1):
                if t < NT:
                    sp.wait_ge(Z["s_h"], t + 1)
                    sp.dma_start(h_d[t * P:(t + 1) * P, :], hh[:, t % 2]).then_inc(Z[f"s_hst{t % 2}"], 16)
                if t + 2 < NT:
                    sp.dma_start(xr[:, t % 2], xv[t + 2]).then_inc(Z[f"s_xr{t % 2}"], 16)
                if t:
                    sp.wait_ge(Z["s_hn2"], t)
                    sp.dma_start(hn2_d[(t - 1) * P:t * P, :], hn2[:, (t - 1) % 2]).then_inc(Z[f"s_nst{(t - 1) % 2}"], 16)

            def piece(src, slot):
                sp.dma_start(raw6[:, slot] if src.shape[1] == 4 else raw6[:, slot].rearrange("p k n -> p (k n)").rearrange("p (k n) -> p k n", k=2),
                             src).then_inc(s_r6[slot], 16)

            def gate_up(e):
                for k in (0, 4):
                    yield egv[e, :, k:k + 4, :] if isinstance(e, int) else egv[bass.ds(e, 1), :, k:k + 4, :].rearrange("a p k n -> (a p) k n")
                    yield euv[e, :, k:k + 4, :] if isinstance(e, int) else euv[bass.ds(e, 1), :, k:k + 4, :].rearrange("a p k n -> (a p) k n")

            def down(e):
                for k in (0, 2):
                    yield edv[e, :, k:k + 2, :] if isinstance(e, int) else edv[bass.ds(e, 1), :, k:k + 2, :].rearrange("a p k n -> (a p) k n")

            sp.wait_ge(Z["s_wo"], NT)
            for n, src in enumerate(gate_up(0)):
                piece(src, n)
            for n, src in enumerate([*gate_up(1)][0:2]):
                piece(src, 4 + n)
            with sp.Fori(0, E // 2 - 1) as i:
                gu = [[*gate_up(i * 2 + k)] for k in (1, 2, 3)]
                for j, src in enumerate([*gu[0][2:4], *down(i * 2), *gu[1], *down(i * 2 + 1), *gu[2][0:2]]):
                    sp.wait_ge(Z["s_plo"], i * 12 + (j + 1))
                    settle(sp)
                    piece(src, j % 6)
            n = 6 * (E - 1)
            for src in [*[*gate_up(E - 1)][2:4], *down(E - 2), *down(E - 1)]:
                sp.wait_ge(Z["s_plo"], n - 5)
                piece(src, n % 6)
                n += 1
            assert n == 6 * E
            sp.wait_ge(Z["s_tabd"], 2)
            nov = sp.value_load(ovt[0:1, 0:1], min_val=0, max_val=NOV)
            with sp.If(nov > 0):
                with sp.Fori(0, NOV) as j:
                    with sp.If(nov > j):
                        e = sp.value_load(ovt[0:1, bass.ds(j + 1, 1)], min_val=0, max_val=E - 1)
                        for k, src in enumerate([*gate_up(e), *down(e)]):
                            sp.wait_ge(Z["s_plo"], j * 6 + (6 * E + k - 5))
                            piece(src, k)
                sp.wait_ge(Z["s_ovd"], 1)

            def residual(t):
                sp.dma_start(hb[:, t % 4], h_d[t * P:(t + 1) * P, :]).then_inc(s_hb[t % 4], 16)

            sp.wait_ge(Z["s_plo"], 6 * E)
            for t in range(4):
                residual(t)
            for t in range(NT):
                sp.wait_ge(Z["s_fin"], t + 1)
                sp.dma_start(outv[t], yo[:, t % 4]).then_inc(s_out[t % 4], 16)
                if t + 4 < NT:
                    residual(t + 4)
            for b in range(4):
                sp.wait_ge(s_out[b], 16 * (NT // 4))

        @block.scalar
        def _(act):
            own = Chain(act, Z["s_act"])

            def do(out_, in_, f, **kw):
                return nc.scalar.activation(out_, in_, f, **kw)

            eps = small[:, 0:1]
            for t in range(NT):
                act.dma_start(xt[:, t], xv[t]).then_inc(Z["s_x"], 16)
            act.wait_ge(Z["s_cols"], 1)
            do(small[:, 8:16], cols[:, C_COND:C_COND + 8], ACT.Silu).then_inc(Z["s_cond"], 1)
            act.wait_ge(Z["s_x"], 16 * NT)
            act.wait_ge(Z["s_const"], 1)
            for t in range(NT):
                if t:
                    act.wait_ge(Z["s_ssq"], t)
                do(win2[:], xt[:, t], ACT.Square, accum_out=small[:, 16 + t:17 + t]).then_inc(Z["s_ssq"], 1)
            act.wait_ge(Z["s_ssq"], NT)
            do(small[:, 24:32], small[:, 16:24], ACT.Sqrt, scale=1.0 / D, bias=eps).then_inc(Z["s_sd"], 1)
            act.wait_ge(Z["s_lbx"], 1)
            do(small[:, 40:48], small[:, 40:48], ACT.Exp).then_inc(Z["s_lbx"], 1)
            for n in range(16):
                hf, k = divmod(n, KC)
                act.wait_ge(Z["s_val"], n + 1)
                do(hnh[:, k, bass.ts(hf, HALF)], valr[:, n % 2], ACT.Copy).then_inc(Z["s_hh"], 1)

            def round_chunk(cn, slot, per_slot):
                act.wait_ge(Z[f"s_raw{slot}"], 32 * per_slot)
                if not (isinstance(cn, int) and cn < 2):
                    act.wait_ge(Z["s_mm"], cn - 1)
                do(wh[:, slot], raw[:, slot], ACT.Copy).then_inc(Z["s_hi"], 1)

            round_chunk(0, 0, 1)
            round_chunk(1, 1, 1)

            def evac(cn, slot, dst, f, **kw):
                act.wait_ge(Z["s_mm"], cn + 1)
                do(dst[:, 0:HALF], A[2 * slot][:, :], f, **kw)
                return do(dst[:, HALF:S], A[2 * slot + 1][:, :], f, **kw)

            def row_vectors(p):
                if p:
                    act.wait_ge(Z["s_rowc"], p)
                    act.dma_start(ada_d[p - 1:p, :], rowr[:]).then_inc(Z["s_rowst"], 16)
                else:
                    act.wait_ge(Z["s_hn"], 16)
                if p < 8:
                    act.dma_start(valr[0:1, 0], b_ada[:, 2 * D + p * HALF:2 * D + (p + 1) * HALF]).then_inc(Z["s_bg"], 16)
                    if gains[p // 2] is not None:
                        act.dma_start(valr[0:1, 1], gains[p // 2][:, (p % 2) * HALF:(p % 2 + 1) * HALF]).then_inc(Z["s_bg"], 16)

            row_vectors(0)
            for cn in range(12):
                kind, j = divmod(cn, 4)
                evac(cn, cn % 2, (Bc, vT, ub)[kind][:, j], ACT.Sigmoid if kind == 0 else ACT.Copy).then_inc(Z["s_free"], 1)
                round_chunk(cn + 2, cn % 2, cn // 2 + 2)
                if cn < 8:
                    row_vectors(cn + 1)
            act.wait_ge(Z["s_B"], 1)
            for j in range(H):
                do(Bc[:, j], Bc[:, j], ACT.Ln).then_inc(Z["s_ln"], 1)
            act.wait_ge(Z["s_acc"], 12)
            with act.Fori(0, 4 // 2) as pair:
                j = pair * 2
                for b in range(2):
                    evac(j + (12 + b), b, Qq[:, bass.ds(j + b, 1)].rearrange("p a n -> p (a n)"), ACT.Silu).then_inc(Z["s_free"], 1)
                    act.wait_ge(Z[f"s_raw{b}"], 32 * 8 + 16 * j)
                    act.wait_ge(Z["s_mm"], j + (13 + b))
                    do(wh[:, b], raw[:, b], ACT.Copy).then_inc(Z["s_hi"], 1)
            for t in range(NT):
                act.wait_ge(Z["s_vt"], t + 1)
                do(Vv[:, t], A[6 + t % 2][:, :], ACT.Copy).then_inc(Z["s_ve"], 1)
            for n in range(8):
                g, hf = divmod(n, 2)
                act.wait_ge(Z["s_pm"], n + 1)
                if n >= 4 and hf == 0:
                    act.wait_ge(Z[f"s_gst{g % 2}"], 16)
                do(pt[:, g % 2, bass.ts(hf, HALF)], A[4 + n % 4][:, :], ACT.Copy,
                   scale=cols[:, C_PS + g:C_PS + g + 1]).then_inc(Z["s_pe"], 1)
                if hf:
                    act.wait_ge(Z["s_pe"], n + 1)
                    act.dma_start(spill[g], pt[:, g % 2]).then_inc(Z[f"s_gst{g % 2}"], 16)
            for j in range(4):
                cn, b = 16 + j, j % 2
                act.wait_ge(Z[f"s_gst{b}"], 16 * (2 + j // 2))
                act.wait_ge(Z["s_mm"], cn + 1)
                do(gt[:, b, 0:HALF], A[2 * b][:, :], ACT.Silu)
                do(gt[:, b, HALF:S], A[2 * b + 1][:, :], ACT.Silu).then_inc(Z["s_free"], 1)
                act.wait_ge(Z["s_free"], cn + 1)
                own.link(do(gt[:, b], gt[:, b], ACT.Copy, scale=cols[:, C_NG + j:C_NG + j + 1]))
                act.dma_start(spill[4 + j], gt[:, b]).then_inc(Z[f"s_gst{b}"], 16)
                round_chunk(cn + 2, b, cn // 2 + 2)

            def gate_evac(t, b):
                act.wait_ge(Z[f"s_gst{b}"], 16 * t + 64)
                act.wait_ge(Z["s_mm"], 2 * t + (N_IN + 1 + b))
                do(gt[:, b, 0:HALF], A[2 * b][:, :], ACT.Copy)
                do(gt[:, b, HALF:S], A[2 * b + 1][:, :], ACT.Copy).then_inc(Z["s_free"], 1)
                act.wait_ge(Z["s_free"], 2 * t + (N_IN + 1 + b))
                act.dma_start(spill[bass.ds(2 * t + (8 + b), 1)].rearrange("a p n -> p (a n)"), gt[:, b]).then_inc(Z[f"s_gst{b}"], 16)

            def gate_round(t, b):
                act.wait_ge(Z[f"s_raw{b}"], 32 * 12 + 32 * t)
                act.wait_ge(Z["s_mm"], 2 * t + (N_IN + 1 + b))
                do(wh[:, b], raw[:, b], ACT.Copy).then_inc(Z["s_hi"], 1)

            def squares(t):
                act.wait_ge(Z["s_o"], t + 1)
                past(act, Z["s_osq"], t)
                for h in range(H):
                    last = do(sqs[:, h], A[6][:, h * P:(h + 1) * P], ACT.Square, accum_out=small[:, 64 + h:65 + h])
                last.then_inc(Z["s_osq"], 1)
                act.wait_ge(Z["s_osq"], t + 1)
                do(small[:, 68:72], small[:, 64:68], ACT.Sqrt, scale=1.0 / P, bias=eps).then_inc(Z["s_osd"], 1)

            def o_high(t):
                act.wait_ge(Z["s_oval"], t + 1)
                settle(act)
                do(oh[:, :, bass.ts(t, P)], ov[:], ACT.Copy).then_inc(Z["s_oh"], 1)

            def tile(t, last_tile):
                tok = bass.ts(t, P)
                do(E0[:], Bc[:, :, tok], ACT.Exp).then_inc(Z["s_E"], 1)
                do(Kc[:], Kk[:, :, tok], ACT.Copy).then_inc(Z["s_kc"], 1)

                def factor(k):
                    act.wait_ge(Z["s_D"], 8 * t + (k + 1))
                    if k == 2:
                        act.wait_ge(Z["s_kd"], t + 1)
                    elif k > 2:
                        act.wait_ge(Z["s_QK"], 7 * t + (k - 2))
                    do(Ee[:, k % 2], Dd[:, k % 2], ACT.Exp).then_inc(Z["s_E"], 1)

                factor(0)
                factor(1)
                if last_tile is not None:
                    gate_round(last_tile, 1)
                    squares(last_tile)
                factor(2)
                act.wait_ge(Z["s_kt"], t + 1)
                do(kdN[:], A[7][:, :].rearrange("p (h n) -> p h n", h=H), ACT.Copy).then_inc(Z["s_kn"], 1)
                factor(3)
                factor(4)
                if last_tile is not None:
                    o_high(last_tile)
                    gate_evac(last_tile, 1)
                for k in range(5, 8):
                    factor(k)
                gate_round(t, 0)
                gate_evac(t, 0)

            act.wait_ge(Z["s_mask"], 1)
            tile(0, None)
            with act.Fori(1, NT) as t:
                tile(t, t - 1)
            squares(NT - 1)
            o_high(NT - 1)
            gate_round(NT - 1, 1)
            gate_evac(NT - 1, 1)

            act.wait_ge(Z["s_mixr"], 32)
            act.wait_ge(Z["s_st"], NT)
            for g in range(H):
                do(mh[:, g], mixr[:, g], ACT.Copy).then_inc(Z["s_mh"], 1)

            biasc = small[:, 4:8].rearrange("p (a b) -> p a b", a=2)

            def branch(m, more):
                past(act, Z["s_sg"], m)
                for a in range(2):
                    own.link(do(biasc[:, a], cols[:, bass.ds(m + (C_BGATE + 8 * a), 2)], ACT.Copy))
                for b in range(2):
                    act.wait_ge(Z[f"s_gl{b}"], 16 * m + 32)
                    do(ghg[:, b], ghg[:, b], ACT.Sigmoid, bias=biasc[:, 0, b:b + 1])
                    do(gpl[:, b], gpl[:, b], ACT.Sigmoid, bias=biasc[:, 1, b:b + 1]).then_inc(Z["s_sg"], 1)
                for b in range(2):
                    for hf in range(2):
                        act.wait_ge(Z["s_bval"], 2 * m + (2 * b + hf + 1))
                        do(hnh[:, bass.ds(m + b, 1), bass.ts(hf, HALF)].rearrange("p a n -> p (a n)"), valr[:, hf], ACT.Copy).then_inc(Z["s_mTh"], 1)
                    if more:
                        act.wait_ge(Z[f"s_raw{b}"], 16 * m + 32 * 20)
                        act.wait_ge(Z["s_mm"], m + (N_A + 1 + b))
                        do(wh[:, b], raw[:, b], ACT.Copy).then_inc(Z["s_hi"], 1)

            branch(0, True)
            with act.Fori(1, KC // 2 - 1) as pair:
                own.enter(pair, 2, 1)
                branch(pair * 2, True)
            own.leave(KC // 2 - 1)
            branch(KC - 2, False)
            act.wait_ge(Z["s_mm"], N_CH)
            for k in range(KC):
                act.wait_ge(s_wraw[k], 16)
                do(woh[:, k], wraw(k), ACT.Copy).then_inc(Z["s_woh"], 1)

            def turned(t):
                for q in range(2):
                    act.wait_ge(Z["s_h2T"], 2 * t + q + 1)
                    if q == 0 and t:
                        act.wait_ge(Z["s_rt"], t)
                    do(h2T[:, 4 * q:4 * q + 4].rearrange("p k n -> p (k n)"), A[4 + q][:, :], ACT.Copy).then_inc(Z["s_h2e"], 1)

            for t in range(NT + 1):
                lo_, hi_ = (82 if t < NT else 83), (84 if t else 83)
                if t < NT:
                    act.wait_ge(Z["s_wo"], t + 1)
                    if t > 1:
                        act.wait_ge(Z["s_hsq"], t - 1)
                    for q in range(2):
                        last = do(junk[:, bass.ts(q, HALF)], A[2 * (t % 2) + q][:, :], ACT.Square, accum_out=small[:, 80 + q:81 + q])
                    last.then_inc(Z["s_mixsq"], 1)
                if t:
                    act.wait_ge(Z["s_mixsq"], min(t + 1, NT))
                    act.wait_ge(Z["s_h"], t)
                    do(junk[:], hh[:, (t - 1) % 2], ACT.Square, accum_out=small[:, 83:84]).then_inc(Z["s_hsq"], 1)
                    act.wait_ge(Z["s_hsq"], t)
                if t < NT:
                    act.wait_ge(Z["s_mixsd"], t + 1)
                do(small[:, lo_ + 2:hi_ + 2], small[:, lo_:hi_], ACT.Sqrt, scale=1.0 / D, bias=eps).then_inc(Z["s_msd"], 1)
                if t >= 2:
                    turned(t - 2)
            turned(NT - 1)

            act.wait_ge(Z["s_ge"], 1)
            do(R[0][:, :, :, 0], R[0][:, :, :, 0], ACT.Exp).then_inc(Z["s_ge"], 1)
            act.wait_ge(Z["s_ge"], 3)
            do(R[2][:, :, 0], R[2][:, :, 0], ACT.Exp).then_inc(Z["s_ge"], 1)

            def hi(turn, slot, free):
                act.wait_ge(s_r6[slot], 16 * turn)
                if free is not None:
                    act.wait_ge(Z["s_pc"], free)
                do(eh[:, slot], raw6[:, slot], ACT.Copy).then_inc(Z["s_phi"], 1)

            def x_high(cnt, b, q):
                act.wait_ge(Z["s_xTp"], 2 * cnt + (q + 1))
                do(xTh[:, b, 4 * q:4 * q + 4].rearrange("p k n -> p (k n)"), A[4][:, :], ACT.Copy).then_inc(Z["s_xTh"], 1)

            def silu(e, b, done):
                act.wait_ge(Z["s_pc"], done)
                if not (isinstance(e, int) and e == 0):
                    act.wait_ge(Z["s_a"], e)
                do(sil[:], A[2 * b][:, :], ACT.Silu).then_inc(Z["s_sil"], 1)

            def a_high(e, b):
                act.wait_ge(Z["s_aT"], e + 1)
                do(aTh[:, b].rearrange("p k n -> p (k n)"), A[5][:, :], ACT.Copy).then_inc(Z["s_aTh"], 1)

            def y_store(e, row, done):
                act.wait_ge(Z["s_pc"], done)
                if not (isinstance(e, int) and e == 0):
                    act.wait_ge(Z["s_yst"], 16 * e)
                do(yy[:, 0:HALF], A[6][:, :], ACT.Copy)
                do(yy[:, HALF:D], A[7][:, :], ACT.Copy).then_inc(Z["s_ycp"], 1)
                act.wait_ge(Z["s_ycp"], e + 1)
                act.dma_start(y_d[row, :], yy[0:BLK, :]).then_inc(Z["s_yst"], 16)

            act.wait_ge(Z["s_rt"], NT)
            for n in range(6):
                hi(1, n, None)
            for e in range(2):
                for q in range(2):
                    x_high(e, e, q)

            def step(e, i, b, first=False, last_x=False):
                n0 = 4 + 6 * (1 - b)

                def h(j):
                    k = n0 + j
                    hi(2 * i + (k // 6 + 1), k % 6, i * 12 + (k - 5))
                silu(e - 1, 1 - b, 4 if first else i * 12 + (n0 - 2))
                h(2)
                h(3)
                if not first:
                    y_store(e - 2, bass.ts(e - 2, BLK), i * 12 + n0)
                if not last_x:
                    x_high(e + 1, 1 - b, 0)
                h(4)
                h(5)
                a_high(e - 1, 1 - b)
                if not last_x:
                    x_high(e + 1, 1 - b, 1)
                h(6)
                h(7)

            step(1, 0, 1, first=True)
            step(2, 0, 0)
            with act.Fori(1, E // 2 - 1) as i:
                step(i * 2 + 1, i, 1)
                step(i * 2 + 2, i, 0)
            step(E - 1, E // 2 - 1, 1, last_x=True)
            silu(E - 1, 1, 6 * E - 4)
            a_high(E - 1, 1)
            y_store(E - 2, bass.ts(E - 2, BLK), 6 * E - 2)
            y_store(E - 1, bass.ts(E - 1, BLK), 6 * E)
            act.wait_ge(Z["s_tabd"], 2)
            nov = act.value_load(ovt[0:1, 0:1], min_val=0, max_val=NOV)
            with act.If(nov > 0):
                with act.Fori(0, NOV) as j:
                    with act.If(nov > j):
                        for q in range(2):
                            x_high(j + E, 0, q)
                        for k in range(6):
                            hi(j + (E + 1), k, j * 6 + (6 * E + k - 5))
                        silu(j + E, 0, j * 6 + (6 * E + 4))
                        a_high(j + E, 0)
                        y_store(j + E, bass.ts(j + E, BLK), j * 6 + (6 * E + 6))
                    with act.If(nov < j + 1):
                        act.dma_start(y_d[bass.ts(j + E, BLK), :], yy[0:BLK, :]).then_inc(Z["s_yst"], 16)
                    act.wait_ge(Z["s_yst"], 16 * j + 16 * (E + 1))
                    settle(act)
            act.wait_ge(Z["s_yst"], 16 * E)
            do(small[:, 121:122], small[:, 0:1], ACT.Copy).then_inc(Z["s_ovd"], 1)
            def first_share(t):
                b = t % 4
                act.wait_ge(s_Y[b], 32 * (t // 4 + 1))
                if t >= 4:
                    act.wait_ge(s_out[b], 16 * (t // 4))
                do(yo[:, b], Y1[:, b], ACT.Copy, scale=wts[:, 0, t:t + 1]).then_inc(Z["s_y1"], 1)

            first_share(0)
            for t in range(NT):
                b = t % 2
                if t + 1 < NT:
                    first_share(t + 1)
                act.wait_ge(Z["s_ysum"], t + 1)
                do(ysq[:], yo[:, t % 4], ACT.Square, accum_out=small[:, 96 + b:97 + b]).then_inc(Z["s_ysq"], 1)
                act.wait_ge(Z["s_ysq"], t + 1)
                do(small[:, 98 + b:99 + b], small[:, 96 + b:97 + b], ACT.Sqrt, scale=1.0 / D, bias=eps).then_inc(Z["s_ysd"], 1)

        @block.tensor
        def _(pe):
            def mm(dst, l, r, start, stop, **kw):
                return nc.tensor.matmul(dst, l, r, start=start, stop=stop, **kw)

            pe.wait_ge(Z["s_ident"], 2)
            pe.wait_ge(Z["s_vec"], 16 * 7)
            nc.tensor.transpose(A[7][:, 0:N_VEC], vecs[:, :], ident[0:N_VEC, 0:N_VEC]).then_inc(Z["s_vecT"], 1)
            pe.wait_ge(Z["s_acc"], 4)
            pe.wait_ge(Z["s_ones"], 1)
            for j in range(16):
                last = mm(A[6][:, j:j + 1], acc0[:, j // 4, (j % 4) * P:(j % 4 + 1) * P], ones[:, 0:1], True, True)
            last.then_inc(Z["s_mod"], 1)
            pe.wait_ge(Z["s_xs"], NT)
            for n in range(16):
                hf, k = divmod(n, KC)
                if n >= 4:
                    pe.wait_ge(Z["s_val"], n - 3)
                for q in range(4):
                    last = nc.tensor.transpose(A[n % 4][:, q * P:(q + 1) * P], xt[:, 4 * hf + q, k * P:(k + 1) * P], ident[:, :])
                last.then_inc(Z["s_xT"], 1)

            def chunk_groups(cn, slot, free):
                pe.wait_ge(Z["s_lo"], cn + 1)
                if free is not None:
                    pe.wait_ge(Z["s_free"], free)
                for hf in range(2):
                    dst = A[2 * slot + hf][:, :]
                    todo = [(l, r, k) for k in range(KC) for l, r in ((wh, hnh), (wh, hnl), (wl, hnh))]
                    for g in range(3):
                        for n, (l, r, k) in enumerate(todo[8 * g:8 * g + 8]):
                            last = mm(dst, l[:, slot, k, :], r[:, k, hf * HALF:(hf + 1) * HALF],
                                      g == 0 and n == 0, g == 2 and n == 7)
                        if hf == 1 and g == 2:
                            last.then_inc(Z["s_mm"], 1)
                        yield

            def chunk(cn, slot, free):
                for _ in chunk_groups(cn, slot, free):
                    pass

            pe.wait_ge(Z["s_hn"], 16)
            pe.wait_ge(Z["s_val"], 16)
            for cn in range(8):
                chunk(cn, cn % 2, cn - 1 if cn >= 2 else None)
                pe.wait_ge(Z["s_acc"], 5 + cn)
                if cn:
                    pe.wait_ge(Z["s_rowc"], cn)
                else:
                    pe.wait_ge(Z["s_modc"], 1)
                mm(A[6][0:1, :], ones[:, 0:1], acc1[:, cn % 2, :], True, True).then_inc(Z["s_adam"], 1)
            with pe.Fori(8 // 2, 16 // 2) as pair:
                cn = pair * 2
                for b in range(2):
                    chunk(cn + b, b, cn + (b - 1))
            pe.wait_ge(Z["s_rowc"], 8)
            for t in range(NT):
                if t >= 2:
                    pe.wait_ge(Z["s_ve"], t - 1)
                for h in range(H):
                    last = nc.tensor.transpose(A[6 + t % 2][:, h * P:(h + 1) * P], vT[:, h, t * P:(t + 1) * P], ident[:, :])
                last.then_inc(Z["s_vt"], 1)
            pe.wait_ge(Z["s_pw"], 16)
            pe.wait_ge(Z["s_ve"], NT)
            for n in range(8):
                g, hf = divmod(n, 2)
                pe.wait_ge(Z["s_pool"], g + 1)
                if n >= 4:
                    pe.wait_ge(Z["s_pe"], n - 3)
                mm(A[4 + n % 4][:, :], poolw[:, g, :], ub[:, g, hf * HALF:(hf + 1) * HALF], True, True).then_inc(Z["s_pm"], 1)
            for cn in range(16, 20):
                chunk(cn, cn % 2, cn - 1)
            pe.wait_ge(Z["s_pe"], 8)

            pe.wait_ge(Z["s_mask"], 1)

            def v_of(t, h):
                return Vv[:, bass.ds(t, 1), h * P:(h + 1) * P].rearrange("p a n -> p (a n)")

            def turn_o(t):
                pe.wait_ge(Z["s_on"], t + 1)
                for h in range(H):
                    last = nc.tensor.transpose(A[7][:, h * P:(h + 1) * P], on[:, h], ident[:, :])
                last.then_inc(Z["s_ot"], 1)

            def tile(t, last_tile):
                tok = bass.ts(t, P)

                def diag():
                    pe.wait_ge(Z["s_kc"], t + 1)
                    past(pe, Z["s_mg"], 8 * t)
                    for h in range(H):
                        last = mm(A[4][:, h * P:(h + 1) * P], Kc[:, h], Qq[:, h, tok], True, True)
                    last.then_inc(Z["s_sc"], 1)

                def turn_k():
                    pe.wait_ge(Z["s_kd"], t + 1)
                    past(pe, Z["s_S"], t)
                    for h in range(H):
                        last = nc.tensor.transpose(A[7][:, h * P:(h + 1) * P], kd[:, h], ident[:, :])
                    last.then_inc(Z["s_kt"], 1)

                def level(k):
                    def go():
                        pe.wait_ge(Z["s_QK"], 7 * t + k)
                        past(pe, Z["s_mg"], 8 * t + (k - 1))
                        for h in range(H):
                            last = mm(A[4 + k % 2][:, h * 64:(h + 1) * 64], KL[:, k % 2, h], QL[:, k % 2, h], True, True)
                        last.then_inc(Z["s_sc"], 1)
                    return go

                def turn_last():
                    if last_tile is not None:
                        pe.wait_ge(Z["s_kn"], t + 1)
                        turn_o(last_tile)

                def outputs():
                    pe.wait_ge(Z["s_mg"], 8 * t + 8)
                    past(pe, Z["s_S"], t)
                    past(pe, Z["s_on"], t)
                    pe.wait_ge(Z["s_qe"], t + 1)
                    for h in range(H):
                        mm(A[6][:, h * P:(h + 1) * P], Sc[:, h], v_of(t, h), True, False)
                        last = mm(A[6][:, h * P:(h + 1) * P], qe[:, h], St[:, h], False, True)
                    last.then_inc(Z["s_o"], 1)
                    pe.wait_ge(Z["s_kn"], t + 1)
                    past(pe, Z["s_oval"], t)
                    for h in range(H):
                        last = mm(A[7][:, h * P:(h + 1) * P], kdN[:, h], v_of(t, h), True, True)
                    last.then_inc(Z["s_st"], 1)

                steps = [diag, turn_k, level(1), level(2), turn_last] + [level(k) for k in range(3, 8)] + [None, outputs]
                n = 0
                for b in range(2):
                    for _ in chunk_groups(2 * t + (N_IN + b), b, 2 * t + (N_IN + b - 1)):
                        if steps[n]:
                            steps[n]()
                        n += 1
                assert n == len(steps)

            tile(0, None)
            with pe.Fori(1, NT) as t:
                tile(t, t - 1)
            turn_o(NT - 1)

            pe.wait_ge(Z["s_oh"], NT)
            pe.wait_ge(Z["s_ol"], NT)
            pe.wait_ge(Z["s_free"], N_A)
            with pe.Fori(0, KC // 2) as pair:
                m = pair * 2
                for b in range(2):
                    pe.wait_ge(Z["s_lo"], m + (N_A + b + 1))
                    for br, (vh, vl) in enumerate(((oh, ol), (mh, ml))):
                        if br:
                            pe.wait_ge(Z["s_ml"], H)
                        for hf in range(2):
                            if br == 0:
                                pe.wait_ge(Z["s_free"], 2 * m + (N_A + 2 * b + hf - 1))
                            cols_ = slice(hf * HALF, (hf + 1) * HALF)
                            todo = [(l, r, k) for k in range(H) for l, r in ((wh, vh), (wh, vl), (wl, vh))]
                            for n, (l, r, k) in enumerate(todo):
                                last = mm(A[2 * hf + br][:, :], l[:, b, 4 * br + k, :], r[:, k, cols_], n == 0, n == 11)
                            if br:
                                last.then_inc(Z["s_mm" if hf else "s_br"], 1)

            pe.wait_ge(Z["s_free"], N_A + 2 * KC)

            def project(t):
                if t >= 2:
                    pe.wait_ge(Z["s_h"], t - 1)
                tk = slice(t * P, (t + 1) * P)
                for k in range(KC):
                    if t == 0:
                        if k in POOL_ROWS:
                            pe.wait_ge(Z["s_wolp"], POOL_ROWS.index(k) + 1)
                        else:
                            pe.wait_ge(Z["s_wolv"], DVE_ROWS.index(k) + 1)
                        pe.wait_ge(Z["s_hn"], 16 + 2 * (k + 1))
                    for n, (l, r) in enumerate(((hnh, woh), (hnh, wol), (hnl, woh))):
                        for q in range(2):
                            last = mm(A[2 * (t % 2) + q][:, :], l[:, k, tk], r[:, k, q * HALF:(q + 1) * HALF],
                                      k == 0 and n == 0, k == KC - 1 and n == 2)
                last.then_inc(Z["s_wo"], 1)

            def turn_hn2(t):
                pe.wait_ge(Z["s_hn2"], t + 1)
                for q in range(2):
                    if t:
                        pe.wait_ge(Z["s_h2e"], 2 * t - 1 + q)
                    for k in range(4):
                        last = nc.tensor.transpose(A[4 + q][:, k * P:(k + 1) * P], hn2[:, t % 2, (4 * q + k) * P:(4 * q + k + 1) * P], ident[:, :])
                    last.then_inc(Z["s_h2T"], 1)

            def route(t):
                pe.wait_ge(Z["s_h2e"], 2 * t + 2)
                pe.wait_ge(Z["s_wr"], 64)
                if t:
                    pe.wait_ge(Z["s_L"], t)
                for k in range(KC):
                    last = mm(A[6][:, 0:G + E], h2T[:, k, :], wr[:, k, :], k == 0, k == KC - 1)
                last.then_inc(Z["s_rt"], 1)

            for t in range(NT + 2):
                if t < NT:
                    project(t)
                if t >= 3:
                    route(t - 3)
                if t >= 2:
                    turn_hn2(t - 2)
            route(NT - 1)

            pe.wait_ge(Z["s_M"], 1)
            Mv = R[7][:].rearrange("p t g e -> p t (g e)")
            pos = A[0][:, 0:NT * E].rearrange("p (t e) -> p t e", e=E)
            pe.wait_ge(Z["s_iota"], 1)
            mm(pos, tri[:], Mv, True, False, skip_group_check=True)
            for s in range(NT - 1):
                last = mm(pos[:, s + 1:, :], ones[:], Mv[:, s:s + 1, :].to_broadcast([P, NT - 1 - s, E]), False, s == NT - 2,
                          skip_group_check=True)
            mm(A[1][:, 0:E], ones[:], c32[:, 0, :], True, True).then_inc(Z["s_pos"], 1)
            for n in range(2 * NT):
                pe.wait_ge(Z["s_AB"], n + 1)
                mm(A[2][0:BLK, 0:NCOL], Aoh[:, n % 2, 0:BLK], Boh[:, n % 2, 0:NCOL], n == 0, n == 2 * NT - 1).then_inc(Z["s_slots"], 1)

            def turn_x(cnt, b, q):
                if q == 0:
                    pe.wait_ge(Z[f"s_xg{b}"], cnt)
                for k in range(4):
                    last = nc.tensor.transpose(A[4][:, k * P:k * P + BLK], xg[0:BLK, b, (4 * q + k) * P:(4 * q + k + 1) * P], ident[0:BLK, 0:BLK])
                last.then_inc(Z["s_xTp"], 1)

            def gate_up_half(n, half, b, w):
                pe.wait_ge(Z["s_plo"], n + 2)
                g, u = A[2 * b][0:BLK, :], A[2 * b + 1][0:BLK, :]
                for k in range(4):
                    kk = 4 * half + k
                    st, sp_ = (kk == 0), (kk == KC - 1)
                    mm(g, xTh[:, b, kk, 0:BLK], eh[:, w[0], k, :], st, False)
                    mm(g, xTh[:, b, kk, 0:BLK], el[:, w[0], k, :], False, False)
                    mm(u, xTh[:, b, kk, 0:BLK], eh[:, w[1], k, :], st, False)
                    mm(u, xTh[:, b, kk, 0:BLK], el[:, w[1], k, :], False, False)
                    lg = mm(g, xTl[:, b, kk, 0:BLK], eh[:, w[0], k, :], False, sp_)
                    lu = mm(u, xTl[:, b, kk, 0:BLK], eh[:, w[1], k, :], False, sp_)
                lg.then_inc(Z["s_pc"], 1)
                lu.then_inc(Z["s_pc"], 1)
                return lu

            def turn_a(e, b):
                pe.wait_ge(Z["s_a"], e + 1)
                if not (isinstance(e, int) and e == 0):
                    pe.wait_ge(Z["s_aTl"], e)
                for k in range(4):
                    last = nc.tensor.transpose(A[5][:, k * P:k * P + BLK], aa[0:BLK, b, k * P:(k + 1) * P], ident[0:BLK, 0:BLK])
                last.then_inc(Z["s_aT"], 1)

            def down(e, n, b, w):
                pe.wait_ge(Z["s_aTl"], e + 1)
                if not (isinstance(e, int) and e == 0):
                    pe.wait_ge(Z["s_ycp"], e)
                for half in range(2):
                    pe.wait_ge(Z["s_plo"], n + (half + 1))
                    for kk in range(2):
                        k = 2 * half + kk
                        for q in range(2):
                            sl = (slice(None), w[half], 2 * kk + q)
                            mm(A[6 + q][0:BLK, :], aTh[:, b, k, 0:BLK], eh[sl], k == 0, False)
                            mm(A[6 + q][0:BLK, :], aTh[:, b, k, 0:BLK], el[sl], False, False)
                            last = mm(A[6 + q][0:BLK, :], aTl[:, b, k, 0:BLK], eh[sl], False, k == 3)
                    last.then_inc(Z["s_pc"], 1)
                return last

            def wait_x(cnt):
                pe.wait_ge(Z["s_xTl"], cnt)

            for e in range(2):
                for q in range(2):
                    if 2 * e + q:
                        wait_x(2 * e + q)
                    turn_x(16, e, q)
            wait_x(2)
            gate_up_half(0, 0, 0, (0, 1))
            gate_up_half(2, 1, 0, (2, 3))

            def pe_step(e, i, b, last_x=False):
                n0 = 4 + 6 * (1 - b)
                w = [(n0 + j) % 6 for j in range(6)]
                if not last_x:
                    wait_x(2 * e + 2)
                    turn_x(i * 16 + 32, 1 - b, 0)
                wait_x(2 * e + 2)
                gate_up_half(i * 12 + n0, 0, b, w[0:2])
                turn_a(e - 1, 1 - b)
                if not last_x:
                    wait_x(2 * e + 3)
                    turn_x(0, 1 - b, 1)
                gate_up_half(i * 12 + (n0 + 2), 1, b, w[2:4])
                down(e - 1, i * 12 + (n0 + 4), 1 - b, w[4:6])

            pe_step(1, 0, 1)
            pe_step(2, 0, 0)
            with pe.Fori(1, E // 2 - 1) as i:
                pe_step(i * 2 + 1, i, 1)
                pe_step(i * 2 + 2, i, 0)
            pe_step(E - 1, E // 2 - 1, 1, last_x=True)
            turn_a(E - 1, 1)
            n = 6 * E - 2
            down(E - 1, n, 1, (n % 6, (n + 1) % 6))
            pe.wait_ge(Z["s_tabd"], 2)
            nov = pe.value_load(ovt[0:1, 0:1], min_val=0, max_val=NOV)
            with pe.If(nov > 0):
                with pe.Fori(0, NOV) as j:
                    with pe.If(nov > j):
                        for q in range(2):
                            wait_x(j * 2 + (2 * E + q))
                            turn_x(16 * j + 16 * (E // 2 + 1), 0, q)
                        wait_x(j * 2 + (2 * E + 2))
                        pe.wait_ge(Z["s_aTl"], j + E)
                        gate_up_half(j * 6 + 6 * E, 0, 0, (0, 1))
                        gate_up_half(j * 6 + (6 * E + 2), 1, 0, (2, 3))
                        turn_a(j + E, 0)
                        down(j + E, j * 6 + (6 * E + 4), 0, (4, 5))

        @block.vector
        def _(dve):
            own = Chain(dve, Z["s_dve"])
            V = nc.vector
            V.memset(small[:, 0:1], EPS).then_inc(Z["s_const"], 1)
            V.memset(ones[:], 1.0).then_inc(Z["s_ones"], 1)
            dve.wait_ge(Z["s_iota"], 1)
            own.link(V.tensor_tensor(xorm[:], iS[:], iT[:], ALU.bitwise_xor))
            own.link(V.tensor_tensor(iS[:], iT[:], iS[:], ALU.is_gt))
            own.link(V.tensor_tensor(xorm[:], xorm[:], iS[:], ALU.mult))
            for n, h in enumerate(LEVELS):
                second = xorm[:].rearrange("p (n b) -> p n b", b=2 * h)[:, :, h:2 * h]
                mk = mask[:, n].rearrange("p (n b) -> p n b", b=h)
                t1 = mtmp[:].rearrange("p (n b) -> p n b", b=h)
                own.link(V.tensor_scalar(t1, second, float(h), None, ALU.is_ge))
                own.link(V.scalar_tensor_tensor(mk, second, float(2 * h), t1, ALU.is_lt, ALU.mult))
            dve.wait_ge(Z["s_vecT"], 1)
            V.tensor_copy(cols[:], A[7][:, 0:N_VEC]).then_inc(Z["s_cols"], 1)
            dve.wait_ge(Z["s_cols"], 1)
            l0, l1 = cols[:, C_LB0:C_LB0 + 4], cols[:, C_LB1:C_LB1 + 4]
            own.link(V.tensor_tensor(small[:, 32:36], l0, l1, ALU.max))
            V.tensor_tensor(small[:, 40:44], l0, small[:, 32:36], ALU.subtract)
            V.tensor_tensor(small[:, 44:48], l1, small[:, 32:36], ALU.subtract).then_inc(Z["s_lbx"], 1)

            dve.wait_ge(Z["s_cond"], 1)

            def ada_piece(dst, slot, turn):
                for k in range(8):
                    if k % 4 == 0:
                        dve.wait_ge(s_ada[slot + k // 4], 16 * turn)
                    src, sc_ = adab[:, slot + k // 4, k % 4, :], small[:, 8 + k:9 + k]
                    if k == 0:
                        own.link(V.tensor_scalar(dst, src, sc_, None, ALU.mult))
                    elif k < 7:
                        own.link(V.scalar_tensor_tensor(dst, src, sc_, dst, ALU.mult, ALU.add))
                    else:
                        V.scalar_tensor_tensor(dst, src, sc_, dst, ALU.mult, ALU.add).then_inc(Z["s_acc"], 1)

            ada_piece(acc0[:, 0], 0, 1)
            ada_piece(acc0[:, 1], 2, 1)
            dve.wait_ge(Z["s_sd"], 1)
            rs = small[:, 48:56]

            def rsqrt(dst, sd, ss, tmp, scale):
                own.link(V.reciprocal(dst, sd))
                own.link(V.tensor_scalar(tmp, ss, scale, EPS, ALU.mult, ALU.add))
                own.link(V.tensor_tensor(tmp, tmp, dst, ALU.mult))
                own.link(V.tensor_tensor(tmp, tmp, dst, ALU.mult))
                own.link(V.tensor_scalar(tmp, tmp, -0.5, 1.5, ALU.mult, ALU.add))
                own.link(V.tensor_tensor(dst, dst, tmp, ALU.mult))

            rsqrt(rs, small[:, 24:32], small[:, 16:24], small[:, 56:64], 1.0 / D)
            for t in range(NT):
                V.tensor_scalar(xt[:, t], xt[:, t], rs[:, t:t + 1], None, ALU.mult).then_inc(Z["s_xs"], 1)
            ada_piece(acc0[:, 2], 0, 2)
            ada_piece(acc0[:, 3], 2, 2)
            dve.wait_ge(Z["s_lbx"], 2)
            own.link(V.tensor_tensor(small[:, 32:36], small[:, 40:44], small[:, 44:48], ALU.add))
            own.link(V.reciprocal(small[:, 32:36], small[:, 32:36]))
            own.link(V.tensor_tensor(small[:, 32:36], small[:, 32:36], small[:, 40:44], ALU.mult))
            own.link(V.tensor_scalar(small[:, 36:40], small[:, 32:36], -1.0, 1.0, ALU.mult, ALU.add))
            dve.wait_ge(Z["s_mod"], 1)
            own.link(V.tensor_tensor(small[:, 72:80], A[6][:, 0:8], cols[:, C_BADA:C_BADA + 8], ALU.add))
            own.link(V.tensor_tensor(small[:, 104:112], A[6][:, 8:16], cols[:, C_BADA + 8:C_BADA + 16], ALU.add))
            V.scalar_tensor_tensor(small[:, 104:112], small[:, 104:112], 1.0, cols[:, C_GPRE:C_GPRE + 8], ALU.add, ALU.mult).then_inc(Z["s_modc"], 1)
            dve.wait_ge(Z["s_modc"], 1)
            dve.wait_ge(Z["s_ssq"], NT)
            for n in range(16):
                k = n % KC
                dve.wait_ge(Z["s_xT"], n + 1)
                if n >= 2:
                    dve.wait_ge(Z["s_hn"], n - 1)
                V.tensor_scalar(valr[:, n % 2], A[n % 4][:, :], small[:, 104 + k:105 + k], small[:, 72 + k:73 + k],
                                ALU.mult, ALU.add).then_inc(Z["s_val"], 1)

            def f_head(j):
                dve.wait_ge(Z["s_free"], j + 1)
                own.link(V.tensor_scalar(Bc[:, j], Bc[:, j], small[:, 36 + j:37 + j], small[:, 32 + j:33 + j], ALU.mult, ALU.add))
                return V.tensor_scalar(Kk[:, j], Bc[:, j], -1.0, 1.0, ALU.mult, ALU.add)

            def row(p):
                gain = gains[p // 2]
                dve.wait_ge(Z["s_adam"], p + 1)
                dve.wait_ge(Z["s_bg"], sum(32 if gains[n // 2] is not None else 16 for n in range(p + 1)))
                if p:
                    dve.wait_ge(Z["s_rowst"], 16 * p)
                biased = V.tensor_tensor(rowr[:], A[6][0:1, :], valr[0:1, 0], ALU.add)
                if gain is None:
                    biased.then_inc(Z["s_rowc"], 1)
                else:
                    own.link(biased)
                    V.scalar_tensor_tensor(rowr[:], rowr[:], 1.0 if gain is g_pre_ffn else 0.0, valr[0:1, 1], ALU.add, ALU.mult).then_inc(Z["s_rowc"], 1)

            ada_piece(acc1[:, 0], 0, 3)
            for p in range(8):
                if p < 4:
                    last = f_head(p)
                    if p == 3:
                        last.then_inc(Z["s_B"], 1)
                if p < 7:
                    row(p)
                    ada_piece(acc1[:, (p + 1) % 2], 2 * ((p + 1) % 2), 3 + (p + 1) // 2)
            row(7)
            dve.wait_ge(Z["s_rowc"], 8)
            dve.wait_ge(Z["s_iota"], 1)
            own.link(V.tensor_scalar(small[:, 128:144], small[:, 128:144], 1.0, None, ALU.add))
            own.link(V.reciprocal(small[:, 128:144], small[:, 128:144]))
            own.link(V.memset(scanm[:], 1.0))
            own.link(V.memset(scanm[:].rearrange("p (t n) -> p t n", n=P)[:, :, 0:1], 0.0))
            dve.wait_ge(Z["s_hn"], 16)
            for g in range(H):
                dve.wait_ge(Z["s_free"], 9 + g)
                u = ub[:, g]
                src, w = u, 1
                for s in range(g + 1):
                    dst = (win1, win2)[s % 2][:]
                    V.tensor_copy(dst[:, 0:w], src[:, 0:w])
                    own.link(V.tensor_tensor(dst[:, w:S], src[:, w:S], src[:, 0:S - w], ALU.add))
                    src, w = dst, 2 * w
                own.link(V.tensor_tensor(src[:, 0:w], src[:, 0:w], small[:, 128:128 + w], ALU.mult))
                V.scalar_tensor_tensor(u[:, w:S], src[:, w:S], 1.0 / w, u[:, w:S], ALU.mult, ALU.subtract)
                V.tensor_tensor(u[:, 0:w], src[:, 0:w], u[:, 0:w], ALU.subtract).then_inc(Z["s_pool"], 1)
                dve.wait_ge(Z["s_pool"], g + 1)
            for j in range(H):
                dve.wait_ge(Z["s_ln"], j + 1)
                own.link(V.tensor_tensor_scan(Bc[:, j], scanm[:], Bc[:, j], 0.0, ALU.mult, ALU.add))
            dve.wait_ge(Z["s_vt"], NT)
            dve.wait_ge(Z["s_pm"], 8)
            dve.wait_ge(Z["s_gst0"], 16 * 2)
            dve.wait_ge(Z["s_gst1"], 16 * 2)
            own.link(V.memset(KL[:], 0.0))
            dve.wait_ge(Z["s_free"], 16)
            V.memset(St[:], 0.0).then_inc(Z["s_mask"], 1)
            dve.wait_ge(Z["s_mask"], 1)

            def state(t):
                dve.wait_ge(Z["s_o"], t + 1)
                dve.wait_ge(Z["s_st"], t + 1)
                dve.wait_ge(Z["s_ebl"], t + 1)
                for h in range(H):
                    last = V.scalar_tensor_tensor(St[:, h], St[:, h], small[:, 112 + h:113 + h], A[7][:, h * P:(h + 1) * P], ALU.mult, ALU.add)
                last.then_inc(Z["s_S"], 1)

            def normalise(t):
                dve.wait_ge(Z["s_osd"], t + 1)
                own.link(V.reciprocal(small[:, 116:120], small[:, 68:72]))
                V.tensor_tensor(on[:], A[6][:, :].rearrange("p (h n) -> p h n", h=H),
                                small[:, 116:120].unsqueeze(2).to_broadcast([P, H, P]), ALU.mult).then_inc(Z["s_on"], 1)

            def gate_o(t):
                dve.wait_ge(Z["s_ot"], t + 1)
                dve.wait_ge(Z["s_gs"], 16 * t + 16)
                past(dve, Z["s_oh"], t)
                V.tensor_tensor(ov[:], A[7][:, :].rearrange("p (h n) -> p h n", h=H), gs[:], ALU.mult).then_inc(Z["s_oval"], 1)

            def o_low(t):
                tok = bass.ts(t, P)
                dve.wait_ge(Z["s_oh"], t + 1)
                V.tensor_tensor(ol[:, :, tok], ov[:], oh[:, :, tok].bitcast(F32), ALU.subtract).then_inc(Z["s_ol"], 1)

            def tile(t, last_tile):
                tok = bass.ts(t, P)
                Bt, Kt, Qt = Bc[:, :, tok], Kk[:, :, tok], Qq[:, :, tok]

                def halves(v, h):
                    w = v.rearrange("p h (n b) -> p h n b", b=2 * h)
                    return w[:, :, :, 0:h], w[:, :, :, h:2 * h], w[:, :, :, h - 1:h].to_broadcast([P, H, 64 // h, h])

                def exponent(k):
                    if k == 0:
                        V.tensor_tensor(Dd[:, 0], Bt[:, :, P - 1:P].to_broadcast([P, H, P]), Bt, ALU.subtract).then_inc(Z["s_D"], 1)
                        return
                    h = LEVELS[k - 1]
                    b1, b2, ref = halves(Bt, h)
                    d1, d2, _ = halves(Dd[:, k % 2], h)
                    V.tensor_tensor(d1, ref, b1, ALU.subtract)
                    V.tensor_tensor(d2, b2, ref, ALU.subtract).then_inc(Z["s_D"], 1)

                def merge(k):
                    dve.wait_ge(Z["s_sc"], 8 * t + (k + 1))
                    if k == 0:
                        past(dve, Z["s_o"], t)
                        V.tensor_tensor(Sc[:], A[4][:, :].rearrange("p (h n) -> p h n", h=H),
                                        ident[:].unsqueeze(1).to_broadcast([P, H, P]), ALU.mult).then_inc(Z["s_mg"], 1)
                        return
                    h = LEVELS[k - 1]
                    dve.wait_ge(Z["s_mg"], 8 * t + k)
                    settle(dve)
                    _, dst, _ = halves(Sc[:], h)
                    V.copy_predicated(dst, mask[:, k - 1].rearrange("p (n b) -> p n b", b=h).unsqueeze(1).to_broadcast([P, H, 64 // h, h]),
                                      A[4 + k % 2][:, 0:H * 64].rearrange("p (h n b) -> p h n b", h=H, b=h)).then_inc(Z["s_mg"], 1)

                def level(k):
                    dve.wait_ge(Z["s_E"], 9 * t + (2 + k))
                    if k == 0:
                        past(dve, Z["s_kt"], t)
                        V.tensor_tensor(kd[:], Kt, Ee[:, 0], ALU.mult).then_inc(Z["s_kd"], 1)
                    else:
                        h = LEVELS[k - 1]
                        past(dve, Z["s_sc"], 8 * t + (k - 1))
                        k1, _, _ = halves(Kt, h)
                        _, q2, _ = halves(Qt, h)
                        e1, e2, _ = halves(Ee[:, k % 2], h)
                        kl1, _, _ = halves(KL[:, k % 2], h)
                        V.tensor_tensor(kl1, k1, e1, ALU.mult)
                        V.tensor_tensor(QL[:, k % 2].rearrange("p h (n b) -> p h n b", b=h), q2, e2, ALU.mult).then_inc(Z["s_QK"], 1)
                    if k + 2 < 8:
                        exponent(k + 2)
                    if k >= 1:
                        merge(k - 1)

                exponent(0)
                exponent(1)
                if last_tile is not None:
                    state(last_tile)
                level(0)
                level(1)
                if last_tile is not None:
                    normalise(last_tile)
                level(2)
                dve.wait_ge(Z["s_E"], 9 * t + 1)
                past(dve, Z["s_o"], t)
                V.tensor_tensor(qe[:], Qt, E0[:], ALU.mult).then_inc(Z["s_qe"], 1)
                V.tensor_copy(small[:, 112:116], E0[:, :, P - 1]).then_inc(Z["s_ebl"], 1)
                level(3)
                if last_tile is not None:
                    gate_o(last_tile)
                level(4)
                level(5)
                if last_tile is not None:
                    o_low(last_tile)
                level(6)
                level(7)
                merge(7)

            tile(0, None)
            with dve.Fori(1, NT) as t:
                own.enter(t, 1, 1)
                tile(t, t - 1)
            own.leave(NT)
            normalise(NT - 1)
            gate_o(NT - 1)
            o_low(NT - 1)

            for g in range(H):
                dve.wait_ge(Z["s_mh"], g + 1)
                V.tensor_tensor(ml[:, g], mixr[:, g], mh[:, g].bitcast(F32), ALU.subtract).then_inc(Z["s_ml"], 1)
            with dve.Fori(0, KC // 2) as pair:
                m = pair * 2
                own.enter(pair, 4)
                for b in range(2):
                    dve.wait_ge(Z["s_sg"], m + (b + 1))
                    for hf in range(2):
                        if hf:
                            dve.wait_ge(Z["s_mm"], m + (N_A + 1 + b))
                        else:
                            dve.wait_ge(Z["s_br"], m + (1 + b))
                        cs = slice(hf * HALF, (hf + 1) * HALF)
                        own.link(V.tensor_tensor(t12[:, 0], A[2 * hf][:, :], ghg[:, b, cs], ALU.mult))
                        V.tensor_tensor(t12[:, 1], A[2 * hf + 1][:, :], gpl[:, b, cs], ALU.mult).then_inc(Z["s_free"], 1)
                        dve.wait_ge(Z["s_free"], 2 * m + (N_A + 2 * b + hf + 1))
                        dve.wait_ge(Z["s_hn"], 2 * m + (16 + 2 * b + hf - 1))
                        V.tensor_tensor(valr[:, hf], t12[:, 0], t12[:, 1], ALU.add).then_inc(Z["s_bval"], 1)
                        dve.wait_ge(Z["s_bval"], 2 * m + (2 * b + hf + 1))
            own.leave(KC // 2)

            for k in DVE_ROWS:
                dve.wait_ge(Z["s_woh"], k + 1)
                V.tensor_tensor(wol[:, k], wraw(k), woh[:, k].bitcast(F32), ALU.subtract).then_inc(Z["s_wolv"], 1)
            dve.wait_ge(Z["s_rowl"], 64)
            dve.wait_ge(Z["s_wr"], 64)

            def logits(t):
                dve.wait_ge(Z["s_rt"], t + 1)
                V.tensor_tensor(L[:, t], A[6][:, 0:G + E], brow[:], ALU.add).then_inc(Z["s_L"], 1)

            for t in range(NT + 1):
                b = t % 2
                lo_, hi_ = (82 if t < NT else 83), (84 if t else 83)
                if t < NT:
                    dve.wait_ge(Z["s_mixsq"], t + 1)
                    V.tensor_tensor(small[:, 82:83], small[:, 80:81], small[:, 81:82], ALU.add).then_inc(Z["s_mixsd"], 1)
                dve.wait_ge(Z["s_msd"], t + 1)
                rsqrt(small[:, lo_ + 4:hi_ + 4], small[:, lo_ + 2:hi_ + 2], small[:, lo_:hi_], small[:, lo_ + 8:hi_ + 8], 1.0 / D)
                if t < NT:
                    if t >= 2:
                        dve.wait_ge(Z["s_hn2"], t - 1)
                    for q in range(2):
                        cs = slice(q * HALF, (q + 1) * HALF)
                        last = V.scalar_tensor_tensor(mm_t[:, cs], A[2 * b + q][:, :], small[:, 86:87], rows[:, 0, cs], ALU.mult, ALU.mult)
                    own.link(last)
                    dve.wait_ge(Z[f"s_xr{b}"], 16 * (t // 2 + 1))
                    if t >= 2:
                        dve.wait_ge(Z[f"s_hst{b}"], 16 * (t // 2))
                    V.tensor_tensor(hh[:, b], mm_t[:], xr[:, b], ALU.add).then_inc(Z["s_h"], 1)
                    dve.wait_ge(Z["s_h"], t + 1)
                if t:
                    c = (t - 1) % 2
                    own.link(V.scalar_tensor_tensor(mm_t[:], hh[:, c], small[:, 87:88], rows[:, 1], ALU.mult, ALU.mult))
                    if t >= 3:
                        dve.wait_ge(Z[f"s_nst{c}"], 16 * ((t - 1) // 2))
                        dve.wait_ge(Z["s_h2T"], 2 * (t - 2))
                    V.tensor_tensor(hn2[:, c], mm_t[:], rows[:, 2], ALU.add).then_inc(Z["s_hn2"], 1)
                if t >= 3:
                    logits(t - 3)
            logits(NT - 2)
            logits(NT - 1)

            dve.wait_ge(Z["s_L"], NT)
            for b in range(2):
                dve.wait_ge(Z[f"s_hst{b}"], 64)
                dve.wait_ge(Z[f"s_nst{b}"], 64)
            dve.wait_ge(Z["s_h2T"], 2 * NT)
            gl = L[:, :, 0:G]
            el_ = L[:, :, G:G + E].rearrange("p t (g e) -> p t g e", e=EG)

            def st(n, k=None):
                return rs_[:, n] if k is None else rs_[:, n, k]

            def bc(v, n):
                return v.unsqueeze(2).to_broadcast([P, NT, n])

            def first_max(prob, n, ramp, best, arg, onehot, tmp):
                own.link(V.tensor_reduce(best, prob, AX.X, ALU.max))
                own.link(V.tensor_tensor(tmp, prob, bc(best, n), ALU.is_ge))
                own.link(V.tensor_scalar(tmp, tmp, -99.0, 99.0, ALU.mult, ALU.add))
                own.link(V.tensor_tensor(tmp, tmp, ramp, ALU.add))
                own.link(V.tensor_reduce(arg, tmp, AX.X, ALU.min))
                own.link(V.tensor_tensor(onehot, ramp, bc(arg, n), ALU.is_equal))

            def softmax_rest(prob, n, total):
                own.link(V.tensor_reduce(total, prob, AX.X, ALU.add))
                own.link(V.reciprocal(total, total))
                own.link(V.tensor_tensor(prob, prob, bc(total, n), ALU.mult))

            gp = R[0][:, :, :, 0]
            own.link(V.tensor_reduce(st(0, 0), gl, AX.X, ALU.max))
            V.tensor_tensor(gp, gl, bc(st(0, 0), G), ALU.subtract).then_inc(Z["s_ge"], 1)
            dve.wait_ge(Z["s_ge"], 2)
            softmax_rest(gp, G, st(0, 0))
            dve.wait_ge(Z["s_iota"], 2)
            rampG = iotaC[:, 0:G].unsqueeze(1).to_broadcast([P, NT, G])
            rampE = iotaC[:, 0:EG].unsqueeze(1).to_broadcast([P, NT, EG])
            ohg = R[1][:, :, :, 0]
            first_max(gp, G, rampG, st(1, 0), st(2, 0), ohg, R[3][:, :, :, 0])
            sel = R[2][:, :, 0]
            own.link(V.tensor_tensor(R[3][:], el_, ohg.unsqueeze(3).to_broadcast([P, NT, G, EG]), ALU.mult))
            own.link(V.tensor_reduce(sel, R[3][:].rearrange("p t g e -> p t e g"), AX.X, ALU.add))
            own.link(V.tensor_reduce(st(3, 0), sel, AX.X, ALU.max))
            V.tensor_tensor(sel, sel, bc(st(3, 0), EG), ALU.subtract).then_inc(Z["s_ge"], 1)
            dve.wait_ge(Z["s_ge"], 4)
            softmax_rest(sel, EG, st(3, 0))
            oh1, oh2, tmp8 = R[4][:, :, 0], R[5][:, :, 0], R[3][:, :, 0]
            first_max(sel, EG, rampE, st(4, 0), st(5, 0), oh1, tmp8)
            own.link(V.scalar_tensor_tensor(sel, oh1, -2.0, sel, ALU.mult, ALU.add))
            first_max(sel, EG, rampE, st(4, 1), st(5, 1), oh2, tmp8)
            own.link(V.tensor_tensor(st(6, 0), st(4, 0), st(4, 1), ALU.add))
            own.link(V.reciprocal(st(6, 0), st(6, 0)))
            for k in range(2):
                own.link(V.tensor_tensor(st(7, k), st(1, 0), st(4, k), ALU.mult))
                own.link(V.tensor_tensor(wts[:, k], st(7, k), st(6, 0), ALU.mult))
                own.link(V.scalar_tensor_tensor(st(8, k), st(2, 0), float(EG), st(5, k), ALU.mult, ALU.add))
            M1, M2, M = R[8], R[9], R[7]
            for Mk, o_ in ((M1, oh1), (M2, oh2)):
                own.link(V.tensor_tensor(Mk[:], ohg.unsqueeze(3).to_broadcast([P, NT, G, EG]),
                                         o_.unsqueeze(2).to_broadcast([P, NT, G, EG]), ALU.mult))
            own.link(V.tensor_tensor(M[:], M1[:], M2[:], ALU.add))
            V.tensor_reduce(c32[:, 0, :], M[:].rearrange("p t g e -> p (g e) t"), AX.X, ALU.add).then_inc(Z["s_M"], 1)
            dve.wait_ge(Z["s_pos"], 1)
            pos = A[0][:, 0:NT * E].rearrange("p (t e) -> p t e", e=E)
            T = R[10][:].rearrange("p t g e -> p t (g e)")
            for k, Mk in enumerate((M1, M2)):
                own.link(V.tensor_tensor(T, pos, Mk[:].rearrange("p t g e -> p t (g e)"), ALU.mult))
                own.link(V.tensor_reduce(st(9, k), T, AX.X, ALU.add))
            own.link(V.memset(st(10), 0.0))
            for j in range(1, NJ + 1):
                own.link(V.scalar_tensor_tensor(st(10), st(9), float(j * BLK), st(10), ALU.is_ge, ALU.add))
            own.link(V.scalar_tensor_tensor(st(11), st(10), float(-BLK), st(9), ALU.mult, ALU.add))
            own.link(V.tensor_copy(c32[:, 1], A[1][:, 0:E]))
            own.link(V.memset(c32[:, 2], 0.0))
            own.link(V.memset(c32[:, 3], 1.0))
            for j in range(1, NJ + 1):
                own.link(V.scalar_tensor_tensor(c32[:, 2], c32[:, 1], float(j * BLK + 1), c32[:, 2], ALU.is_ge, ALU.add))
            own.link(V.tensor_tensor_scan(c32[:, 5], c32[:, 3], c32[:, 2], 0.0, ALU.mult, ALU.add))
            own.link(V.tensor_tensor(c32[:, 4], c32[:, 5], c32[:, 2], ALU.subtract))
            for k, Mk in enumerate((M1, M2)):
                own.link(V.tensor_tensor(T, Mk[:].rearrange("p t g e -> p t (g e)"), c32[:, 4:5, :].to_broadcast([P, NT, E]), ALU.mult))
                own.link(V.tensor_reduce(st(12, k), T, AX.X, ALU.add))
            own.link(V.tensor_tensor(st(13), st(12), st(10), ALU.add))
            own.link(V.tensor_scalar(st(13), st(13), float(E - 1), None, ALU.add))
            own.link(V.tensor_tensor(st(13), st(13), st(8), ALU.subtract))
            own.link(V.tensor_scalar(st(14), st(10), 1.0, None, ALU.is_ge))
            own.link(V.tensor_tensor(st(13), st(13), st(14), ALU.mult))
            own.link(V.tensor_tensor(st(13), st(13), st(8), ALU.add))
            own.link(V.scalar_tensor_tensor(st(15), st(13), float(BLK), st(11), ALU.mult, ALU.add))
            own.link(V.tensor_copy(dest[:], st(15)))
            own.link(V.tensor_copy(ovt[0:1, 0:1], c32[0:1, 5, E - 1:E]))
            own.link(V.tensor_tensor(ovcmp[0:1], c32[0:1, 5:6, :].to_broadcast([1, NOV, E]),
                                     iotaC[0:1, 0:NOV].unsqueeze(2).to_broadcast([1, NOV, E]), ALU.is_le))
            own.link(V.tensor_reduce(ovf[0:1, 0:NOV], ovcmp[0:1], AX.X, ALU.add))
            own.link(V.tensor_scalar(ovf[0:1, 0:NOV], ovf[0:1, 0:NOV], float(E - 1), None, ALU.min))
            V.tensor_copy(ovt[0:1, 1:1 + NOV], ovf[0:1, 0:NOV]).then_inc(Z["s_tabd"], 1)
            for n in range(2 * NT):
                t, k = divmod(n, 2)
                if n >= 2:
                    dve.wait_ge(Z["s_slots"], n - 1)
                V.tensor_scalar(Aoh[:, n % 2], iotaS[:], rs_[:, 11, k, t:t + 1], None, ALU.is_equal)
                V.tensor_scalar(Boh[:, n % 2], iotaC[:], rs_[:, 13, k, t:t + 1], small[:, 148 + t:149 + t], ALU.is_equal, ALU.mult).then_inc(Z["s_AB"], 1)
            dve.wait_ge(Z["s_slots"], 2 * NT)
            V.tensor_copy(idxt[0:BLK, 0:NCOL], A[2][0:BLK, 0:NCOL]).then_inc(Z["s_tabd"], 1)

            def lo(n, slot):
                dve.wait_ge(Z["s_phi"], n + 1)
                V.tensor_tensor(el[:, slot], raw6[:, slot], eh[:, slot].bitcast(F32), ALU.subtract).then_inc(Z["s_plo"], 1)

            def x_low(cnt, b, q):
                dve.wait_ge(Z["s_xTh"], 2 * cnt + (q + 1))
                V.tensor_tensor(xTl[:, b, 4 * q:4 * q + 4].rearrange("p k n -> p (k n)"), A[4][:, :],
                                xTh[:, b, 4 * q:4 * q + 4].rearrange("p k n -> p (k n)").bitcast(F32), ALU.subtract).then_inc(Z["s_xTl"], 1)

            def a_prod(e, b):
                dve.wait_ge(Z["s_sil"], e + 1)
                V.tensor_tensor(aa[:, b], A[2 * b + 1][:, :], sil[:], ALU.mult).then_inc(Z["s_a"], 1)

            def a_low(e, b):
                dve.wait_ge(Z["s_aTh"], e + 1)
                V.tensor_tensor(aTl[:, b].rearrange("p k n -> p (k n)"), A[5][:, :],
                                aTh[:, b].rearrange("p k n -> p (k n)").bitcast(F32), ALU.subtract).then_inc(Z["s_aTl"], 1)

            for n in range(6):
                lo(n, n)
            for e in range(2):
                for q in range(2):
                    x_low(e, e, q)

            def step(e, i, b, last_x=False):
                n0 = 4 + 6 * (1 - b)

                def l_(j):
                    k = n0 + j
                    lo(i * 12 + k, k % 6)
                a_prod(e - 1, 1 - b)
                l_(2)
                l_(3)
                if not last_x:
                    x_low(e + 1, 1 - b, 0)
                l_(4)
                l_(5)
                a_low(e - 1, 1 - b)
                if not last_x:
                    x_low(e + 1, 1 - b, 1)
                l_(6)
                l_(7)

            with dve.Fori(0, E // 2 - 1) as i:
                step(i * 2 + 1, i, 1)
                step(i * 2 + 2, i, 0)
            step(E - 1, E // 2 - 1, 1, last_x=True)
            a_prod(E - 1, 1)
            a_low(E - 1, 1)
            nov = dve.value_load(ovt[0:1, 0:1], min_val=0, max_val=NOV)
            with dve.If(nov > 0):
                with dve.Fori(0, NOV) as j:
                    with dve.If(nov > j):
                        for q in range(2):
                            x_low(j + E, 0, q)
                        for k in range(6):
                            lo(j * 6 + (6 * E + k), k)
                        a_prod(j + E, 0)
                        a_low(j + E, 0)

            def second_share(t):
                dve.wait_ge(Z["s_y1"], t + 1)
                dve.wait_ge(s_Y[t % 4], 32 * (t // 4 + 1))
                V.scalar_tensor_tensor(yo[:, t % 4], Y2[:, t % 4], wts[:, 1, t:t + 1], yo[:, t % 4], ALU.mult, ALU.add).then_inc(Z["s_ysum"], 1)

            second_share(0)
            for t in range(NT):
                b = t % 2
                if t + 1 < NT:
                    second_share(t + 1)
                dve.wait_ge(Z["s_ysd"], t + 1)
                rsqrt(small[:, 100:101], small[:, 98 + b:99 + b], small[:, 96 + b:97 + b], small[:, 101:102], 1.0 / D)
                V.scalar_tensor_tensor(yo[:, t % 4], yo[:, t % 4], small[:, 100:101], rows[:, 3], ALU.mult, ALU.mult).then_inc(Z["s_yn"], 1)
                dve.wait_ge(Z["s_yn"], t + 1)

        @block.gpsimd
        def _(pool):
            own = Chain(pool, Z["s_pool_own"])
            PL = nc.gpsimd
            PL.memset(ident[:], 0.0).then_inc(Z["s_ident"], 1)
            pool.wait_ge(Z["s_ident"], 1)
            PL.affine_select(out=ident[:], in_=ident[:], compare_op=ALU.not_equal, fill=1.0, base=0,
                             pattern=[[-1, P]], channel_multiplier=1).then_inc(Z["s_ident"], 1)
            own.link(PL.iota(small[:, 128:144], pattern=[[1, 16]], base=0, channel_multiplier=0, allow_small_or_imprecise_dtypes=True))
            own.link(PL.iota(small[:, 148:156], pattern=[[P, NT]], base=0, channel_multiplier=1, allow_small_or_imprecise_dtypes=True))
            own.link(PL.iota(iS[:], pattern=[[0, P]], base=0, channel_multiplier=1))
            PL.iota(iT[:], pattern=[[1, P]], base=0, channel_multiplier=0).then_inc(Z["s_iota"], 1)

            for n in range(16):
                hf, k = divmod(n, KC)
                pool.wait_ge(Z["s_hh"], n + 1)
                PL.tensor_tensor(hnl[:, k, bass.ts(hf, HALF)], valr[:, n % 2], hnh[:, k, bass.ts(hf, HALF)].bitcast(F32),
                                 ALU.subtract).then_inc(Z["s_hn"], 1)

            def low(cn, b):
                pool.wait_ge(Z["s_hi"], cn + 1)
                PL.tensor_tensor(wl[:, b], raw[:, b], wh[:, b].bitcast(F32), ALU.subtract).then_inc(Z["s_lo"], 1)

            with pool.Fori(0, N_A // 2) as pair:
                cn = pair * 2
                for b in range(2):
                    low(cn + b, b)
            low(N_A, 0)
            low(N_A + 1, 1)

            def branch(m, more):
                for b in range(2):
                    for hf in range(2):
                        pool.wait_ge(Z["s_mTh"], 2 * m + (2 * b + hf + 1))
                        dst = (slice(None), bass.ds(m + b, 1), bass.ts(hf, HALF))
                        PL.tensor_tensor(hnl[dst].rearrange("p a n -> p (a n)"), valr[:, hf],
                                         hnh[dst].rearrange("p a n -> p (a n)").bitcast(F32), ALU.subtract).then_inc(Z["s_hn"], 1)
                    if more:
                        low(m + (N_A + 2 + b), b)

            with pool.Fori(0, KC // 2 - 1) as pair:
                branch(pair * 2, True)
            branch(KC - 2, False)
            for k in POOL_ROWS:
                pool.wait_ge(Z["s_woh"], k + 1)
                PL.tensor_tensor(wol[:, k], wraw(k), woh[:, k].bitcast(F32), ALU.subtract).then_inc(Z["s_wolp"], 1)
            pool.wait_ge(Z["s_hn2"], NT)
            for b in range(2):
                pool.wait_ge(Z[f"s_hst{b}"], 64)
                pool.wait_ge(Z[f"s_nst{b}"], 64)
            pool.wait_ge(Z["s_h2T"], 2 * NT)
            own.link(PL.iota(iotaS[:], pattern=[[1, P]], base=0, channel_multiplier=0, allow_small_or_imprecise_dtypes=True))
            own.link(PL.iota(iotaC[:], pattern=[[1, 64]], base=0, channel_multiplier=0, allow_small_or_imprecise_dtypes=True))
            own.link(PL.memset(tri[:], 1.0))
            PL.affine_select(out=tri[:], in_=tri[:], compare_op=ALU.is_gt, fill=0.0, base=0, pattern=[[1, P]],
                             channel_multiplier=-1).then_inc(Z["s_iota"], 1)

            pool.wait_ge(Z["s_tabd"], 2)

            def gather(cnt, col, b):
                PL.tensor_copy(idxc[0:BLK, b], idxt[0:BLK, col]).then_inc(Z["s_idx"], 1)
                pool.wait_ge(Z["s_idx"], cnt + 1)
                settle(pool)
                PL.indirect_dma_start(out=xg[0:BLK, b], out_offset=None, in_=hn2_d[:, :],
                                      in_offset=bass.IndirectOffsetOnAxis(ap=idxc[0:BLK, b], axis=0)).then_inc(Z[f"s_xg{b}"], 16)

            gather(0, slice(0, 1), 0)
            gather(1, slice(1, 2), 1)
            with pool.Fori(0, E // 2 - 1) as i:
                for b in range(2):
                    e = i * 2 + (2 + b)
                    pool.wait_ge(Z["s_xTp"], 4 * i + (2 * b + 2))
                    gather(e, bass.ds(e, 1), b)
            nov = pool.value_load(ovt[0:1, 0:1], min_val=0, max_val=NOV)
            with pool.If(nov > 0):
                with pool.Fori(0, NOV) as j:
                    with pool.If(nov > j):
                        pool.wait_ge(Z["s_xTp"], j * 2 + 2 * E)
                        gather(j + E, bass.ds(j + E, 1), 0)
            pool.wait_ge(Z["s_ovd"], 1)

            def rows_of(source):
                def look_up(t):
                    for k, Y in enumerate((Y1, Y2)):
                        PL.indirect_dma_start(out=Y[:, t % 4], out_offset=None, in_=source,
                                              in_offset=bass.IndirectOffsetOnAxis(ap=dest[:, k, t:t + 1], axis=0)).then_inc(s_Y[t % 4], 16)

                for t in range(4):
                    look_up(t)
                for t in range(NT):
                    if t + 4 < NT:
                        pool.wait_ge(Z["s_ysum"], t + 1)
                        look_up(t + 4)
                    pool.wait_ge(Z["s_yn"], t + 1)
                    pool.wait_ge(s_hb[t % 4], 16 * (t // 4 + 1))
                    PL.tensor_tensor(yo[:, t % 4], yo[:, t % 4], hb[:, t % 4], ALU.add).then_inc(Z["s_fin"], 1)

            with pool.If(nov > 0):
                rows_of(y_d[:, :])
            with pool.If(nov < 1):
                rows_of(y_d[0:E * BLK, :])


_INS = ['x', 'c', 'w_ada', 'b_ada', 'g_pre_mix', 'g_post_mix', 'w_in', 'hg_lb_logits', 'hg_norm_g', 'pool_w', 'pool_scale',
        'w_branch_hg', 'w_branch_pool', 'w_gate', 'b_gate', 'w_out', 'g_pre_ffn', 'g_post_ffn', 'w_router_group',
        'b_router_group', 'w_router_expert', 'b_router_expert', 'w_exp_gate', 'w_exp_up', 'w_exp_down']
_OUTS = [((1, 1024, 1024), 'float32')]


def kernel(**inputs):
    import numpy as _np
    import concourse.bacc as _bacc
    from concourse import mybir as _mybir
    from concourse.bass_utils import run_bass_kernel_spmd as _run

    nc = _bacc.Bacc("TRN2", target_bir_lowering=False, num_devices=1)
    arrays, args = {}, []
    for name in _INS:
        a = _np.ascontiguousarray(inputs[name])
        arrays[f"in_{name}_dram"] = a
        args.append(nc.dram_tensor(f"in_{name}_dram", a.shape, _mybir.dt.from_np(a.dtype), kind="ExternalInput").ap())
    for i, (shape, dtype) in enumerate(_OUTS):
        dt = _mybir.dt.from_np(_np.dtype(dtype))
        args.append(nc.dram_tensor(f"out_{i}_dram", shape, dt, kind="ExternalOutput").ap())
    build(nc, *args)
    r = _run(nc, [arrays], core_ids=[0])
    got = tuple(r.results[0][f"out_{i}_dram"] for i in range(len(_OUTS)))
    return got[0]
```
